# Optimizing a Trainium2 kernel written in Bass

```python
import jax, jax.numpy as jnp
from jax import lax
import numpy as np

D_MODEL = 1024
BATCH = 1
SEQ = 512
DEPTH = 1

HEAD_DIM = 64
A_Q_HEADS = 8
A_KV_HEADS = 2
A_GROUP = A_Q_HEADS // A_KV_HEADS
B_GROUPS = ((128, 1), (512, 4), (2048, 16))
B_HEADS_PER_GROUP = 4
B_HEADS = B_HEADS_PER_GROUP * len(B_GROUPS)
GRID_W = 64
ROPE_THETA = 10000.0
Q_BLOCK = 128
N_EXPERTS = 16
EXPERT_FF = 1024
EC_CAPACITY_FACTOR = 2
NORM_EPS = 1e-6
NEG_INF = -1e30

A_Q_W = A_Q_HEADS * HEAD_DIM
A_KV_W = A_KV_HEADS * HEAD_DIM
B_W = B_HEADS * HEAD_DIM
B_OUT_W = B_HEADS_PER_GROUP * HEAD_DIM
N_IN = A_Q_W + 2 * A_KV_W + 3 * B_W + 2 * D_MODEL

kernel_name = "hybrid_gqa2drope_dilated_alibi_ecmoe"

def rms_norm(x, g):
    xf = x.astype(jnp.float32)
    y = xf * lax.rsqrt(jnp.mean(xf * xf, axis=-1, keepdims=True) + NORM_EPS)
    return (y * g.astype(jnp.float32)).astype(x.dtype)

def axial_rope_tables(seq):
    rows = seq // GRID_W
    row_id = jnp.repeat(jnp.arange(rows, dtype=jnp.float32), GRID_W)
    col_id = jnp.tile(jnp.arange(GRID_W, dtype=jnp.float32), rows)
    half = HEAD_DIM // 2
    inv_freq = 1.0 / (ROPE_THETA ** (jnp.arange(0, half, 2, dtype=jnp.float32) / half))
    ang_r = row_id[:, None] * inv_freq[None, :]
    ang_c = col_id[:, None] * inv_freq[None, :]
    return (jnp.cos(ang_r)[:, None, :], jnp.sin(ang_r)[:, None, :],
            jnp.cos(ang_c)[:, None, :], jnp.sin(ang_c)[:, None, :])

def _rotate(x, cos, sin):
    n = x.shape[-1] // 2
    x1, x2 = x[..., :n], x[..., n:]
    return jnp.concatenate([x1 * cos - x2 * sin, x2 * cos + x1 * sin], axis=-1)

def apply_axial_rope(x, tables):
    cos_r, sin_r, cos_c, sin_c = tables
    xf = x.astype(jnp.float32)
    half = HEAD_DIM // 2
    out = jnp.concatenate([_rotate(xf[..., :half], cos_r, sin_r),
                           _rotate(xf[..., half:], cos_c, sin_c)], axis=-1)
    return out.astype(x.dtype)

def axial_gqa_attention(q, k, v, q_g, k_g):
    bsz, seq, _ = q.shape
    q = rms_norm(q.reshape(bsz, seq, A_Q_HEADS, HEAD_DIM), q_g)
    k = rms_norm(k.reshape(bsz, seq, A_KV_HEADS, HEAD_DIM), k_g)
    v = v.reshape(bsz, seq, A_KV_HEADS, HEAD_DIM)
    tables = axial_rope_tables(seq)
    q = apply_axial_rope(q, tables) * (HEAD_DIM ** -0.5)
    k = apply_axial_rope(k, tables)
    q = q.reshape(bsz, seq, A_KV_HEADS, A_GROUP, HEAD_DIM)

    def block(s0):
        qb = lax.dynamic_slice_in_dim(q, s0, Q_BLOCK, axis=1)
        s = jnp.einsum('bqkgd,bskd->bkgqs', qb, k).astype(jnp.float32)
        p = jax.nn.softmax(s, axis=-1).astype(v.dtype)
        return jnp.einsum('bkgqs,bskd->bqkgd', p, v)

    starts = jnp.arange(seq // Q_BLOCK, dtype=jnp.int32) * Q_BLOCK
    o = lax.map(block, starts)
    return jnp.moveaxis(o, 0, 1).reshape(bsz, seq, A_Q_W)

def dilated_window_attention(q, k, v):
    bsz, seq, _ = q.shape
    n_g = len(B_GROUPS)
    q = q.reshape(bsz, seq, n_g, B_HEADS_PER_GROUP, HEAD_DIM) * (HEAD_DIM ** -0.5)
    k = k.reshape(bsz, seq, n_g, B_HEADS_PER_GROUP, HEAD_DIM)
    v = v.reshape(bsz, seq, n_g, B_HEADS_PER_GROUP, HEAD_DIM)
    qs = [q[:, :, gi] for gi in range(n_g)]
    ks = [k[:, :, gi] for gi in range(n_g)]
    vs = [v[:, :, gi] for gi in range(n_g)]
    slopes = jnp.exp2(-8.0 * jnp.arange(1, B_HEADS + 1, dtype=jnp.float32) / B_HEADS)
    slopes = slopes.reshape(n_g, B_HEADS_PER_GROUP)

    def block(s0):
        t = s0 + jnp.arange(Q_BLOCK, dtype=jnp.int32)
        outs, lses = [], []
        for gi, (window, dil) in enumerate(B_GROUPS):
            n_side = window // (2 * dil)
            off = np.arange(-n_side, n_side + 1, dtype=np.int32) * dil
            idx = t[:, None] + jnp.asarray(off)[None, :]
            valid = (idx >= 0) & (idx < seq)
            idxc = jnp.clip(idx, 0, seq - 1)
            qb = lax.dynamic_slice_in_dim(qs[gi], s0, Q_BLOCK, axis=1)
            kg = ks[gi][:, idxc]
            vg = vs[gi][:, idxc]
            s = jnp.einsum('bqhd,bqkhd->bhqk', qb, kg).astype(jnp.float32)
            s = s - slopes[gi][:, None, None] * jnp.abs(jnp.asarray(off, jnp.float32))[None, None, :]
            s = jnp.where(valid[None, None], s, NEG_INF)
            lse = jax.nn.logsumexp(s, axis=-1)
            p = jnp.exp(s - lse[..., None]).astype(vg.dtype)
            outs.append(jnp.einsum('bhqk,bqkhd->bqhd', p, vg))
            lses.append(lse)
        w = jax.nn.softmax(jnp.stack(lses, axis=0), axis=0)
        w = jnp.swapaxes(w, 2, 3)[..., None]
        o = jnp.sum(jnp.stack(outs, axis=0).astype(jnp.float32) * w, axis=0)
        return o.astype(v.dtype)

    starts = jnp.arange(seq // Q_BLOCK, dtype=jnp.int32) * Q_BLOCK
    o = lax.map(block, starts)
    return jnp.moveaxis(o, 0, 1).reshape(bsz, seq, B_OUT_W)

def expert_choice_swiglu(h, w_router, w_gate, w_up, w_down):
    bsz, seq, dm = h.shape
    cap = EC_CAPACITY_FACTOR * seq // N_EXPERTS
    aff = jax.nn.softmax(jnp.einsum('bsd,de->bse', h, w_router).astype(jnp.float32), axis=-1)
    g, idx = lax.top_k(jnp.swapaxes(aff, 1, 2), cap)
    xin = jax.vmap(lambda hb, ib: hb[ib])(h, idx)
    a = jnp.einsum('becd,edf->becf', xin, w_gate)
    u = jnp.einsum('becd,edf->becf', xin, w_up)
    y = jnp.einsum('becf,efd->becd', jax.nn.silu(a) * u, w_down) * g[..., None].astype(h.dtype)
    return jax.vmap(lambda ib, yb: jnp.zeros((seq, dm), yb.dtype).at[ib.reshape(-1)].add(yb.reshape(-1, dm)))(idx, y)

def setup_inputs(seed: int = 0) -> dict:
    key = jax.random.key(seed)
    ks = jax.random.split(key, 16)
    f32 = jnp.float32
    nrm = lambda k, shape, fan_in: jax.random.normal(k, shape, f32) * (fan_in ** -0.5)
    gain = lambda k, shape: 1.0 + 0.02 * jax.random.normal(k, shape, f32)
    return {
        "x": jax.random.normal(ks[0], (BATCH, SEQ, D_MODEL), f32),
        "norm1_g": gain(ks[1], (DEPTH, D_MODEL)),
        "w_in": nrm(ks[2], (DEPTH, D_MODEL, N_IN), D_MODEL),
        "b_gates": 0.1 * jax.random.normal(ks[3], (DEPTH, 2 * D_MODEL), f32),
        "q_norm_g": gain(ks[4], (DEPTH, HEAD_DIM)),
        "k_norm_g": gain(ks[5], (DEPTH, HEAD_DIM)),
        "w_o_a": nrm(ks[6], (DEPTH, A_Q_W, D_MODEL), A_Q_W),
        "w_o_b": nrm(ks[7], (DEPTH, B_OUT_W, D_MODEL), B_OUT_W),
        "w_out": nrm(ks[8], (DEPTH, D_MODEL, D_MODEL), D_MODEL),
        "norm2_g": gain(ks[9], (DEPTH, D_MODEL)),
        "w_router": nrm(ks[10], (DEPTH, D_MODEL, N_EXPERTS), D_MODEL),
        "w_gate": nrm(ks[11], (DEPTH, N_EXPERTS, D_MODEL, EXPERT_FF), D_MODEL),
        "w_up": nrm(ks[12], (DEPTH, N_EXPERTS, D_MODEL, EXPERT_FF), D_MODEL),
        "w_down": nrm(ks[13], (DEPTH, N_EXPERTS, EXPERT_FF, D_MODEL), EXPERT_FF),
        "normf_g": gain(ks[14], (D_MODEL,)),
    }

def reference(x, norm1_g, w_in, b_gates, q_norm_g, k_norm_g, w_o_a, w_o_b, w_out,
              norm2_g, w_router, w_gate, w_up, w_down, normf_g):
    splits = np.cumsum([A_Q_W, A_KV_W, A_KV_W, B_W, B_W, B_W, D_MODEL])
    for l in range(DEPTH):
        h = rms_norm(x, norm1_g[l])
        z = jnp.einsum('bsd,dn->bsn', h, w_in[l])
        qa, ka, va, qb, kb, vb, ga, gb = jnp.split(z, splits, axis=-1)
        gate_a = jax.nn.sigmoid(ga + b_gates[l, :D_MODEL])
        gate_b = jax.nn.sigmoid(gb + b_gates[l, D_MODEL:])
        ya = jnp.einsum('bsc,cd->bsd', axial_gqa_attention(qa, ka, va, q_norm_g[l], k_norm_g[l]), w_o_a[l])
        yb = jnp.einsum('bsc,cd->bsd', dilated_window_attention(qb, kb, vb), w_o_b[l])
        x = x + jnp.einsum('bsc,cd->bsd', gate_a * ya + gate_b * yb, w_out[l])
        x = x + expert_choice_swiglu(rms_norm(x, norm2_g[l]), w_router[l], w_gate[l], w_up[l], w_down[l])
    return rms_norm(x, normf_g)


_drawn_inputs = setup_inputs


def setup_inputs(seed=0):
    import zlib

    import numpy as np

    out = dict(_drawn_inputs(seed))
    spreads = {}
    factors = {'norm1_g': 7.175,
     'b_gates': 7.675,
     'q_norm_g': 8.0,
     'k_norm_g': 8.0,
     'norm2_g': 3.278,
     'normf_g': 2.876}
    for name, (base, spread) in spreads.items():
        noise = np.random.default_rng([zlib.crc32(name.encode()), seed]).standard_normal(out[name].shape)
        drawn = base * np.exp(spread * noise) if base else spread * noise
        out[name] = __import__('jax').numpy.asarray(drawn.astype(out[name].dtype))
    for name, factor in factors.items():
        out[name] = (out[name] * factor).astype(out[name].dtype)
    return out
```

```python
import math
from contextlib import ExitStack

import numpy as np

import concourse.bass as bass
from concourse import mybir

ALU = mybir.AluOpType
ACT = mybir.ActivationFunctionType
F32 = mybir.dt.float32
F32R = mybir.dt.float32r
AX = mybir.AxisListType.X

P = 128
SEQ = 512
D = 1024
NT = SEQ // P
KC = D // P
HD = 64
A_HEADS, A_KV = 8, 2
B_GROUPS = ((128, 1), (512, 4), (2048, 16))
NG = len(B_GROUPS)
B_HPG = 4
B_HEADS = NG * B_HPG
A_Q_W, A_KV_W, B_W = A_HEADS * HD, A_KV * HD, B_HEADS * HD
NE = 16
FF = 1024
CAP = 2 * SEQ // NE
EPS = 1e-6
GRID_W = 64
ROPE_THETA = 10000.0
FAR = 1e32
KIB = 1024

COL_A = 0
COL_BQ = A_Q_W + 2 * A_KV_W
COL_BK = COL_BQ + B_W
COL_BV = COL_BK + B_W
COL_GA = COL_BV + B_W
COL_GB = COL_GA + D
RING = 4
SCALE = HD ** -0.5
SLOPES = [2.0 ** (-8.0 * (i + 1) / B_HEADS) for i in range(B_HEADS)]


def strips_in_order():
    out = [("a", i) for i in range((A_Q_W + 2 * A_KV_W) // P)]
    out += [("v", i) for i in range(B_W // P)]
    for hp in range(B_HPG // 2):
        out += [(kind, g, hp) for kind in "qk" for g in range(NG)]
    for j in range(KC):
        out += [("ga", j), ("gb", j), ("wo", j)]
    return out + [("out", i) for i in range(D // P)]


def encoder_block(nc, x, norm1_g, w_in, b_gates, q_norm_g, k_norm_g, w_o_a, w_o_b, w_out, norm2_g,
                  w_router, w_gate, w_up, w_down, normf_g, identity, rope, distance, slots, out):
    strips = strips_in_order()
    at = {s: n for n, s in enumerate(strips)}
    w_in_k = w_in[0].rearrange("(k p) n -> p k n", p=P)
    w_oa_k = w_o_a[0].rearrange("(k p) n -> p k n", p=P)
    w_ob_k = w_o_b[0].rearrange("(k p) n -> p k n", p=P)
    w_out_k = w_out[0].rearrange("(k p) n -> p k n", p=P)
    x_t = x[0].rearrange("(i c) d -> i c d", c=NT)
    out_t = out[0].rearrange("(i c) d -> i c d", c=NT)
    OA, OB = A_Q_W // P, B_HPG * HD // P

    base = (nc.sbuf_base + 31) // 32 * 32

    def sb(name, shape, kib, dt=F32):
        return nc.alloc_sbuf_tensor_at(name, [P] + shape, dt, offset=base + int(kib * KIB))

    hT_hi = sb("hT_hi", [KC, SEQ], 0, F32R)
    hT_lo = sb("hT_lo", [KC, SEQ], 16, F32R)
    w_raw = sb("w_raw", [RING, KC, P], 32)
    w_hi = sb("w_hi", [RING, KC, P], 48, F32R)
    w_lo = sb("w_lo", [RING, KC, P], 64, F32R)
    oT_hi = sb("oT_hi", [OA + OB, SEQ], 80, F32R)
    oT_lo = sb("oT_lo", [OA + OB, SEQ], 92, F32R)
    ident = sb("ident", [P], 104)
    small = sb("small", [256], 104.5)
    rope_t = sb("rope_t", [2, 2, NT, HD], 105.5)
    stage_e = sb("stage_e", [2, SEQ], 105.5)
    W0 = 111.5
    x_in = sb("x_in", [NT, D], W0)
    rope_in = sb("rope_in", [2, NT, HD], W0 + 16)
    t1 = sb("t1", [A_HEADS + A_KV, HD], W0 + 18)
    t2 = sb("t2", [A_HEADS + A_KV, HD], W0 + 20.5)
    pT = sb("pT", [2, NT, SEQ], W0)
    pT_dil = sb("pT_dil", [2, 2, SEQ], W0 + 16)
    probs = sb("probs", [2, SEQ + 2 * P], W0 + 24)
    dist = sb("dist", [NT + 1, SEQ], W0 + 30)
    vB = sb("vB", [NT, B_W], W0 + 40)
    vA = sb("vA", [NT, A_KV_W], W0 + 52)
    zA = sb("zA", [NT, A_HEADS + A_KV, HD], W0 + 54)
    q_parts = sb("q_parts", [2, A_HEADS, 2, HD], W0, F32R)
    k_parts = sb("k_parts", [2, A_KV, 3, HD], W0 + 8, F32R)
    squares = sb("squares", [D], W0 + 54)
    qA = sb("qA", [A_HEADS, SEQ], W0 + 70, F32R)
    kA = sb("kA", [A_KV, 2, SEQ], W0 + 86, F32R)
    qB = sb("qB", [2, NG, SEQ], W0 + 54, F32R)
    kB = sb("kB", [2, NG, 2, SEQ], W0 + 66, F32R)
    m_a = sb("m_a", [SEQ], W0 + 48)
    m_b = sb("m_b", [SEQ], W0 + 50)
    mT_hi = sb("mT_hi", [KC, SEQ], W0 + 64, F32R)
    mT_lo = sb("mT_lo", [KC, SEQ], W0 + 80, F32R)
    x2 = sb("x2", [NT, D], 80)
    xn_hi = sb("xn_hi", [NT, D], 0, F32R)
    xn_lo = sb("xn_lo", [NT, D], 16, F32R)
    xn = sb("xn", [NT, D], 32)
    h2T = sb("h2T", [KC, SEQ], 48)
    w_rt = sb("w_rt", [KC, NE], 64)
    logitT = sb("logitT", [SEQ], 65)
    logit = sb("logit", [NT, NE], 67)
    affT = sb("affT", [SEQ], 68)
    left = sb("left", [2, SEQ], 70)
    best = sb("best", [CAP], 74)
    taken = sb("taken", [SEQ], 75)
    count = sb("count", [SEQ], 77)
    zeros = sb("zeros", [SEQ], 65)
    aff = sb("aff", [NT, NE], 96)
    pos = sb("pos", [NT, NE], 96.25)
    slot_id = sb("slot_id", [CAP], 96.5)
    HALF = KC // 2
    wslot = [sb(f"wslot{i}", [HALF, D], W0 + 16 * i) for i in range(6)]
    pick = sb("pick", [NT, 4, CAP], 32, F32R)
    pick_g = sb("pick_g", [NT, 4, CAP], 36)
    give = sb("give", [2, SEQ], 40)
    xinT = sb("xinT", [KC, 4 * CAP], 44)
    sig = sb("sig", [SEQ], 52)
    act = sb("act", [SEQ], 54)
    actT = sb("actT", [NT, P], 56)
    yE = sb("yE", [D], 58)
    gf = sb("gf", [D], 97)
    fin = sb("fin", [NT, D], 32)

    g1, g2 = small[:, 0:8], small[:, 8:16]
    bg = small[:, 16:32]
    ssq, rstd = small[:, 32:36], small[:, 36:40]
    neg_half = small[:, 40:80]
    ssqA, rstdA = small[:, 80:120], small[:, 120:160]
    nmax, rsum, rinv = small[:, 160:162], small[:, 162:164], small[:, 164:166]
    smax, ssum, sinv = small[:, 168:172], small[:, 172:176], small[:, 176:180]
    gq, gk = sb("gq", [HD], W0 + 64), sb("gk", [HD], W0 + 64.25)

    with ExitStack() as ctx:
        def sem(name):
            return ctx.enter_context(nc.semaphore(name))

        bank = [ctx.enter_context(nc.psum_tensor(f"bank{i}", [P, 512], F32)) for i in range(8)]
        pp = bank[0:4]
        tp = bank[4:8]

        consts_in = sem("consts_in")
        x_tile_in = [sem(f"x_tile_in{c}") for c in range(NT)]
        x_again_in = sem("x_again_in")
        dist_in = sem("dist_in")
        w_raw_in = [sem(f"w_raw_in{i}") for i in range(RING)]
        w_split = sem("w_split")
        w_hi_done = sem("w_hi_done")
        neg_half_set = sem("neg_half_set")
        sumsq_done = sem("sumsq_done")
        ms_done = sem("ms_done")
        rstd_done = sem("rstd_done")
        x_normed = sem("x_normed")
        x_turned = sem("x_turned")
        hT_hi_done = sem("hT_hi_done")
        hT_lo_done = sem("hT_lo_done")
        proj_done = sem("proj_done")
        proj_read_act = sem("proj_read_act")
        proj_read_dve = sem("proj_read_dve")
        dve_step = sem("dve_step")
        a_sumsq = sem("a_sumsq")
        a_ms = sem("a_ms")
        a_rstd = sem("a_rstd")
        a_parts = sem("a_parts")
        a_turned = sem("a_turned")
        a_turned_read = sem("a_turned_read")
        score_done = sem("score_done")
        score_read = sem("score_read")
        nmax_done = sem("nmax_done")
        exp_done = sem("exp_done")
        probs_normed = sem("probs_normed")
        probs_turned = sem("probs_turned")
        pT_done = sem("pT_done")
        pv_done = sem("pv_done")
        o_hi_done = sem("o_hi_done")
        o_lo_done = sem("o_lo_done")
        col_hi_done = sem("col_hi_done")
        branch_done = sem("branch_done")
        gates_used = sem("gates_used")
        merged = sem("merged")
        silu_half = sem("silu_half")
        m_hi_done = sem("m_hi_done")
        m_lo_done = sem("m_lo_done")
        w_slot_in = [sem(f"w_slot_in{i}") for i in range(6)]
        w_slot_used = [sem(f"w_slot_used{i}") for i in range(6)]
        router_in = sem("router_in")
        sumsq2 = sem("sumsq2")
        rstd2 = sem("rstd2")
        xn_done = sem("xn_done")
        xn_hi_done = sem("xn_hi_done")
        xn_lo_done = sem("xn_lo_done")
        xn_turned = sem("xn_turned")
        h2T_done = sem("h2T_done")
        logits_done = sem("logits_done")
        logits_read = sem("logits_read")
        route_turned = sem("route_turned")
        route_read = sem("route_read")
        smax_done = sem("smax_done")
        sexp_done = sem("sexp_done")
        aff_done = sem("aff_done")
        pos_done = sem("pos_done")
        pick_done = sem("pick_done")
        gathered = sem("gathered")
        xin_done = sem("xin_done")
        give_turned = sem("give_turned")
        give_done = sem("give_done")
        sig_done = sem("sig_done")
        act_done = sem("act_done")
        act_turned = sem("act_turned")
        actT_done = sem("actT_done")
        y_done = sem("y_done")
        scattered = sem("scattered")
        added = sem("added")
        ssq3 = sem("ssq3")
        rstd3 = sem("rstd3")
        fin_done = sem("fin_done")
        out_written = sem("out_written")

        groups = [("tok", kind, p, c) for kind in "av" for p in range(3) for c in range(NT)]
        groups += [("col",) + s for s in strips if s[0] in "qk"]
        groups += [("gate", j, b) for j in range(KC) for b in range(2)]
        groups += [("res", p, c) for p in range(D // P // 2) for c in range(NT)]
        g_at = {g: n for n, g in enumerate(groups)}
        by_act = [g[0] in ("tok", "gate") for g in groups]

        NA = A_HEADS * NT
        N_RES = D // P // 2 * NT
        N_COL = 2 * NG * 2
        N_TOK = 6 * NT

        def wait_used(eng, n):
            kind, i = strips[n][0:2]
            if kind in "av":
                eng.wait_ge(proj_done, g_at[("tok", kind, i // 2, NT - 1)] + 1)
            elif kind in "qk":
                eng.wait_ge(proj_done, g_at[("col",) + strips[n]] + 1)
            elif kind == "wo":
                eng.wait_ge(branch_done, 2 * (i + 1))
            elif kind == "out":
                eng.wait_ge(proj_done, g_at[("res", i // 2, NT - 1)] + 1)
            else:
                eng.wait_ge(proj_done, g_at[("gate", i, int(kind == "gb"))] + 1)

        block = ctx.enter_context(nc.Block())

        @block.sync
        def _(sp):
            for c in range(NT):
                sp.dma_start(x_in[:, c, :], x_t[:, c, :]).then_inc(x_tile_in[c], 16)

            def load_strip(n):
                s = strips[n]
                if n >= RING:
                    sp.wait_ge(w_split, n - RING + 1)
                raw = w_raw[:, n % RING]
                done = w_raw_in[n % RING]
                if s[0] == "wo":
                    cols = slice(P * s[1], P * (s[1] + 1))
                    sp.dma_start(raw[:, 0:OA, :], w_oa_k[:, :, cols]).then_inc(done, 16)
                    sp.dma_start(raw[:, OA:OA + OB, :], w_ob_k[:, :, cols]).then_inc(done, 16)
                    return
                if s[0] == "out":
                    sp.dma_start(raw, w_out_k[:, :, P * s[1]:P * (s[1] + 1)]).then_inc(done, 16)
                    return
                if s[0] == "q":
                    col = COL_BQ + (s[1] * B_HPG + 2 * s[2]) * HD
                elif s[0] == "k":
                    col = COL_BK + (s[1] * B_HPG + 2 * s[2]) * HD
                else:
                    col = {"a": COL_A, "v": COL_BV, "ga": COL_GA, "gb": COL_GB}[s[0]] + P * s[1]
                sp.dma_start(raw, w_in_k[:, :, col:col + P]).then_inc(done, 16)

            def load_slot(i, e):
                rows = (w_gate, w_up, w_down)[i // 2][0, e].rearrange("(h k p) n -> h p k n", h=2, p=P)[i % 2]
                sp.dma_start(wslot[i][:, :, :], rows).then_inc(w_slot_in[i], 16)

            for n in range(len(strips)):
                load_strip(n)
                if strips[n] == ("gb", 1):
                    sp.wait_ge(pv_done, OA + OB)
                    for i in range(3):
                        load_slot(i, 0)
            sp.wait_ge(branch_done, 2 * KC)
            sp.dma_start(x2[:, :, :], x_t).then_inc(x_again_in, 16)
            sp.wait_ge(m_hi_done, KC)
            sp.wait_ge(m_lo_done, KC)
            load_slot(3, 0)
            sp.wait_ge(proj_done, len(groups))
            sp.dma_start(w_rt[:, :, :], w_router[0].rearrange("(k p) e -> p k e", p=P)).then_inc(router_in, 16)
            for i in (4, 5):
                load_slot(i, 0)
            with sp.Fori(1, NE) as e:
                for i in range(6):
                    sp.wait_ge(w_slot_used[i], e)
                    load_slot(i, e)
            for c in range(NT):
                sp.wait_ge(fin_done, c + 1)
                sp.dma_start(out_t[:, c, :], fin[:, c, :]).then_inc(out_written, 16)
            sp.wait_ge(out_written, 16 * NT)

        @block.gpsimd
        def _(pool):
            pool.memset(neg_half, -0.5).then_inc(neg_half_set, 1)
            pool.wait_ge(neg_half_set, 1)

            def power(sums, into, n, width, counted, done, first):
                pool.tensor_scalar(into, sums, 1.0 / width, EPS, ALU.mult, ALU.add).then_inc(counted, 1)
                pool.wait_ge(counted, first + 1)
                pool.tensor_tensor(into, into, neg_half[:, 0:n], ALU.pow).then_inc(done, 1)

            for c in range(NT):
                pool.wait_ge(sumsq_done, c + 1)
                power(ssq[:, c:c + 1], rstd[:, c:c + 1], 1, D, ms_done, rstd_done, c)

            for n, s in enumerate(strips):
                if n == at[("v", 4)]:
                    w = A_HEADS + A_KV
                    for c in range(NT):
                        pool.wait_ge(a_sumsq, c + 1)
                        power(ssqA[:, w * c:w * c + w], rstdA[:, w * c:w * c + w], w, HD, a_ms, a_rstd, c)
                k = OA + OB if s[0] == "wo" else KC
                arrived = sum(2 if t[0] == "wo" else 1 for t in strips[n % RING:n + 1:RING])
                pool.wait_ge(w_raw_in[n % RING], 16 * arrived)
                if n >= RING:
                    wait_used(pool, n - RING)
                raw, hi, lo = (w[:, n % RING, 0:k, :] for w in (w_raw, w_hi, w_lo))
                pool.tensor_scalar(hi, raw, 1.0, 1.0, ALU.mult, ALU.mult).then_inc(w_hi_done, 1)
                pool.wait_ge(w_hi_done, n + 1)
                pool.tensor_tensor(lo, raw, hi.bitcast(F32), ALU.subtract).then_inc(w_split, 1)

            for c in range(NT):
                pool.wait_ge(sumsq2, c + 1)
                power(ssq[:, c:c + 1], rstd[:, c:c + 1], 1, D, ms_done, rstd2, NT + c)
            for c in range(NT):
                pool.wait_ge(ssq3, c + 1)
                power(ssq[:, c:c + 1], rstd[:, c:c + 1], 1, D, ms_done, rstd3, 2 * NT + c)

        @block.scalar
        def _(act_):
            for dst, src in ((ident[:, :], identity), (rope_in[:, :, :, :], rope)):
                act_.dma_start(dst, src).then_inc(consts_in, 16)
            for dst, src in ((g1, norm1_g[0]), (g2, norm2_g[0]), (bg, b_gates[0])):
                act_.dma_start(dst, src.rearrange("(k p) -> p k", p=P),
                               allow_slow_non_contiguous=True).then_inc(consts_in, 16)
            for dst, src in ((gq, q_norm_g), (gk, k_norm_g)):
                act_.dma_start(dst[:, :], src[0].partition_broadcast(P)).then_inc(consts_in, 16)

            for c in range(NT):
                act_.wait_ge(x_tile_in[c], 16)
                if c:
                    act_.wait_ge(sumsq_done, c)
                act_.activation(squares[:, :], x_in[:, c, :], ACT.Square,
                                accum_out=ssq[:, c:c + 1]).then_inc(sumsq_done, 1)
            act_.dma_start(dist[:, :, :], distance).then_inc(dist_in, 16)
            act_.wait_ge(consts_in, 16 * 7)
            for k in range(KC):
                act_.wait_ge(x_turned, k + 1)
                act_.activation(hT_hi[:, k, :], bank[k][:, :], ACT.Copy, scale=g1[:, k:k + 1])\
                    .then_inc(hT_hi_done, 1)

            def read_tok(kind, p, c):
                n = g_at[("tok", kind, p, c)]
                src = pp[n % 4][:, 0:2 * P]
                act_.wait_ge(proj_done, n + 1)
                if kind == "v":
                    act_.activation(vB[:, c, 2 * P * p:2 * P * (p + 1)], src, ACT.Copy)\
                        .then_inc(proj_read_act, 1)
                elif p < 2:
                    act_.activation(zA[:, c, 4 * p:4 * p + 4, :], src.rearrange("p (h d) -> p h d", d=HD),
                                    ACT.Copy).then_inc(proj_read_act, 1)
                else:
                    act_.activation(zA[:, c, 8:10, :], src[:, 0:P].rearrange("p (h d) -> p h d", d=HD), ACT.Copy)
                    act_.activation(vA[:, c, :], src[:, P:2 * P], ACT.Copy).then_inc(proj_read_act, 1)

            def read_turned(c):
                for b in range(3):
                    n = 3 * c + b
                    act_.wait_ge(a_turned, n + 1)
                    src = tp[n % 4][:, :].rearrange("p (h i) -> p h i", i=P)
                    cols = slice(P * c, P * c + P)
                    if b < 2:
                        act_.activation(qA[:, 4 * b:4 * b + 4, cols], src, ACT.Copy, scale=SCALE)\
                            .then_inc(a_turned_read, 1)
                    else:
                        dst = kA[:, :, :, cols].rearrange("p k v i -> p (k v) i")
                        act_.activation(dst, src, ACT.Copy).then_inc(a_turned_read, 1)

            for kind, p in (("a", 0), ("a", 1), ("a", 2), ("v", 0), ("v", 1)):
                for c in range(NT):
                    read_tok(kind, p, c)
            read_turned(0)
            read_tok("v", 2, 0)
            read_tok("v", 2, 1)
            read_turned(1)
            read_tok("v", 2, 2)
            read_tok("v", 2, 3)
            read_turned(2)
            read_turned(3)

            def soft_exp(u, width, src):
                act_.wait_ge(nmax_done, u + 1)
                if u >= 2:
                    act_.wait_ge(probs_turned, u - 1)
                act_.activation(probs[:, u % 2, 0:width], src, ACT.Exp, bias=nmax[:, u % 2:u % 2 + 1],
                                accum_out=rsum[:, u % 2:u % 2 + 1]).then_inc(exp_done, 1)

            def read_probs(u):
                head, c = divmod(u, NT)
                cols = slice(P * c, P * c + P)
                if head >= 2:
                    act_.wait_ge(pv_done, head // 2)
                act_.wait_ge(probs_turned, u + 1)
                last = act_.activation(pT[:, head % 2, :, cols],
                                       tp[(0, 3)[u % 2]][:, :].rearrange("p (k i) -> p k i", i=P), ACT.Copy)
                if u >= NA:
                    last = act_.activation(pT_dil[:, head % 2, :, cols],
                                           tp[1][:, 0:2 * P].rearrange("p (g i) -> p g i", i=P), ACT.Copy)
                last.then_inc(pT_done, 1)

            def read_o(i):
                act_.wait_ge(pv_done, i + 1)
                act_.activation(oT_hi[:, i, :], tp[2][:, :], ACT.Copy).then_inc(o_hi_done, 1)

            for u in range(NA + 1):
                if u < NA:
                    soft_exp(u, SEQ, pp[u % 2][:, :])
                if u >= 1:
                    read_probs(u - 1)
                if u >= 9 and u % 8 == 1:
                    read_o(u // 8 - 1)
            read_o(OA - 1)

            for hp in range(2):
                for kind in "qk":
                    for g in range(NG):
                        n = g_at[("col", kind, g, hp)]
                        act_.wait_ge(proj_done, n + 1)
                        src = pp[n % 4]
                        for hh in range(2):
                            half = slice(HD * hh, HD * hh + HD)
                            other = slice(HD - HD * hh, 2 * HD - HD * hh)
                            if kind == "q":
                                last = act_.activation(qB[half, hh, g, :], src[half, :], ACT.Copy, scale=SCALE)
                            else:
                                act_.activation(kB[half, hh, g, 0, :], src[half, :], ACT.Copy)
                                last = act_.activation(kB[other, hh, g, 1, :], src[half, :], ACT.Copy)
                        last.then_inc(col_hi_done, 1)
                first, end = NA + 2 * NT * hp, NA + 2 * NT * (hp + 1)
                for u in range(first, end + 1):
                    if u < end:
                        soft_exp(u, SEQ + 2 * P, probs[:, u % 2, :])
                    if u > first:
                        read_probs(u - 1)
                read_o(OA + hp)

            for j in range(KC):
                for b in range(2):
                    n = g_at[("gate", j, b)]
                    act_.wait_ge(proj_done, n + 1)
                    if j:
                        act_.wait_ge(gates_used, 2 * j)
                    act_.activation(stage_e[:, b, :], pp[n % 4][:, :], ACT.Sigmoid,
                                    bias=bg[:, KC * b + j:KC * b + j + 1]).then_inc(proj_read_act, 1)
                act_.wait_ge(merged, j + 1)
                act_.activation(mT_hi[:, j, :], m_a[:, :], ACT.Copy).then_inc(m_hi_done, 1)

            act_.wait_ge(proj_read_dve, N_COL + N_RES)
            for c in range(NT):
                act_.activation(xn[:, c, :], x2[:, c, :], ACT.Square,
                                accum_out=ssq[:, c:c + 1]).then_inc(sumsq2, 1)
            act_.dma_start(gf[:, :], normf_g.partition_broadcast(P)).then_inc(router_in, 16)
            act_.dma_start(slot_id[:, :], slots).then_inc(router_in, 16)
            for c in range(NT):
                act_.wait_ge(xn_done, c + 1)
                act_.activation(xn_hi[:, c, :], xn[:, c, :], ACT.Copy).then_inc(xn_hi_done, 1)
            for k in range(KC):
                act_.wait_ge(xn_turned, k + 1)
                act_.activation(h2T[:, k, :], bank[k][:, :], ACT.Copy, scale=g2[:, k:k + 1])\
                    .then_inc(h2T_done, 1)
            act_.wait_ge(logits_done, 1)
            act_.activation(logitT[0:NE, :], bank[0][0:NE, :], ACT.Copy).then_inc(logits_read, 1)
            act_.wait_ge(smax_done, 1)
            for c in range(NT):
                act_.activation(logit[:, c, :], bank[1][:, NE * c:NE * c + NE], ACT.Exp,
                                bias=smax[:, c:c + 1], accum_out=ssum[:, c:c + 1]).then_inc(sexp_done, 1)

            with act_.Fori(0, NE // 4) as q:
                for b in range(4):
                    act_.wait_ge(gathered, 4 * q + (b + 1))
                    for j in range(2):
                        k = 2 * b + j
                        last = act_.activation(xinT[:, k, :], bank[4 + b % 2][:, 4 * CAP * j:4 * CAP * (j + 1)],
                                               ACT.Copy, scale=g2[:, k:k + 1])
                    last.then_inc(xin_done, 1)
                for i in range(4):
                    act_.wait_ge(w_slot_used[1], 4 * q + (i + 1))
                    if i:
                        act_.wait_ge(act_done, 4 * q + i)
                    act_.activation(sig[:, :], bank[0][:, :], ACT.Sigmoid).then_inc(sig_done, 1)
                    act_.wait_ge(act_turned, 4 * q + (i + 1))
                    act_.activation(actT[:, :, :], bank[2][:, :].rearrange("p (k i) -> p k i", i=P), ACT.Copy)\
                        .then_inc(actT_done, 1)
                    act_.wait_ge(w_slot_used[5], 4 * q + (i + 1))
                    rows = slice(CAP * (i % 2), CAP * (i % 2) + CAP)
                    act_.activation(yE[rows, 0:SEQ], bank[3][0:CAP, :], ACT.Copy)
                    act_.activation(yE[rows, SEQ:D], bank[3][CAP:2 * CAP, :], ACT.Copy).then_inc(y_done, 1)
                    if i % 2:
                        act_.wait_ge(scattered, 16 * q + 8 * (i // 2 + 1))

            for c in range(NT):
                act_.wait_ge(added, NE // 2 * 8 + 1)
                act_.activation(fin[:, c, :], x2[:, c, :], ACT.Square,
                                accum_out=ssq[:, c:c + 1]).then_inc(ssq3, 1)

        @block.tensor
        def _(pe):
            def split_product(out_, k, n_k, stat, mov):
                (s_hi, s_lo), (m_hi, m_lo) = stat, mov
                pe.matmul(out_, s_hi, m_hi, start=(k == 0), stop=False)
                pe.matmul(out_, s_hi, m_lo, start=False, stop=False)
                return pe.matmul(out_, s_lo, m_hi, start=False, stop=(k == n_k - 1))

            pe.wait_ge(consts_in, 16 * 7)
            for c in range(NT):
                pe.wait_ge(x_normed, c + 1)
                for k in range(KC):
                    t = pe.transpose(bank[k][:, P * c:P * c + P], x_in[:, c, P * k:P * k + P], ident[:, :])
                    if c == NT - 1:
                        t.then_inc(x_turned, 1)

            def pp_take(n):
                if n >= 4:
                    m = n - 4
                    if by_act[m]:
                        pe.wait_ge(proj_read_act, sum(by_act[:m + 1]))
                    else:
                        pe.wait_ge(proj_read_dve, m + 1 - sum(by_act[:m + 1]))

            def tok_group(group, n0, act_parts):
                n, c = g_at[group], group[-1]
                pe.wait_ge(w_split, n0 + 2)
                pp_take(n)
                s = n0 % RING
                cols = slice(P * c, P * c + P)
                for k in range(KC):
                    mm = split_product(pp[n % 4][:, 0:2 * P], k, KC, [t[:, k, cols] for t in act_parts],
                                       [w[:, s:s + 2, k, :] for w in (w_hi, w_lo)])
                mm.then_inc(proj_done, 1)

            def col_group(group, n0):
                n = g_at[group]
                pe.wait_ge(w_split, n0 + 1)
                pp_take(n)
                for k in range(KC):
                    mm = split_product(pp[n % 4][:, :], k, KC, [w[:, n0 % RING, k, :] for w in (w_hi, w_lo)],
                                       [t[:, k, :] for t in (hT_hi, hT_lo)])
                mm.then_inc(proj_done, 1)

            def turn_a(c):
                pe.wait_ge(a_parts, c + 1)
                for b in range(3):
                    n = 3 * c + b
                    if n >= 4:
                        pe.wait_ge(a_turned_read, n - 3)
                    for i in range(4):
                        src = q_parts[:, c % 2, 4 * b + i, :, :] if b < 2 else \
                            k_parts[:, c % 2, i // 2, i % 2:i % 2 + 2, :]
                        t = pe.transpose(tp[n % 4][:, P * i:P * i + P],
                                         src.rearrange("p a d -> p (a d)").bitcast(F32), ident[:, :])
                    t.then_inc(a_turned, 1)

            pe.wait_ge(hT_lo_done, KC)
            hT = (hT_hi, hT_lo)
            for kind, p in (("a", 0), ("a", 1), ("a", 2), ("v", 0), ("v", 1)):
                for c in range(NT):
                    tok_group(("tok", kind, p, c), at[(kind, 2 * p)], hT)
            turn_a(0)
            tok_group(("tok", "v", 2, 0), at[("v", 4)], hT)
            tok_group(("tok", "v", 2, 1), at[("v", 4)], hT)
            turn_a(1)
            tok_group(("tok", "v", 2, 2), at[("v", 4)], hT)
            tok_group(("tok", "v", 2, 3), at[("v", 4)], hT)
            turn_a(2)
            turn_a(3)

            def scores_a(u):
                h, c = divmod(u, NT)
                if u >= 2:
                    pe.wait_ge(exp_done, u - 1)
                for v in range(2):
                    mm = pe.matmul(pp[u % 2][:, :], qA[:, h, P * c:P * c + P],
                                   kA[:, h // (A_HEADS // A_KV), v, :], start=(v == 0), stop=(v == 1))
                mm.then_inc(score_done, 1)

            def scores_b(u):
                head, c = divmod(u - NA, NT)
                cols = slice(P * c, P * c + P)
                if u >= NA + 2:
                    pe.wait_ge(score_read, u - NA - 1)
                for g in range(NG):
                    dst = pp[u % 2][:, :] if g == 0 else pp[2 + u % 2][:, P * (g - 1):P * g]
                    for v in range(2):
                        keys = kB[:, head % 2, g, v, :] if g == 0 else kB[:, head % 2, g, v, cols]
                        mm = pe.matmul(dst, qB[:, head % 2, g, cols], keys, start=(v == 0), stop=(v == 1))
                mm.then_inc(score_done, 1)

            def turn_probs(u):
                pe.wait_ge(probs_normed, u + 1)
                if u >= NA:
                    pe.wait_ge(pT_done, u)
                    for g in range(2):
                        pe.transpose(tp[1][:, P * g:P * g + P],
                                     probs[:, u % 2, SEQ + P * g:SEQ + P * g + P], ident[:, :])
                elif u >= 2:
                    pe.wait_ge(pT_done, u - 1)
                for k in range(NT):
                    t = pe.transpose(tp[(0, 3)[u % 2]][:, P * k:P * k + P],
                                     probs[:, u % 2, P * k:P * k + P], ident[:, :])
                t.then_inc(probs_turned, 1)

            def values_a(i):
                pe.wait_ge(pT_done, 2 * NT * (i + 1))
                if i:
                    pe.wait_ge(o_lo_done, i)
                kv = 2 * i // (A_HEADS // A_KV)
                for k in range(NT):
                    for hh in range(2):
                        mm = pe.matmul(tp[2][HD * hh:HD * hh + HD, :], vA[:, k, HD * kv:HD * kv + HD],
                                       pT[:, hh, k, :], start=(k == 0), stop=(k == NT - 1))
                mm.then_inc(pv_done, 1)

            def values_b(hp):
                pe.wait_ge(pT_done, NA + 2 * NT * (hp + 1))
                pe.wait_ge(o_lo_done, OA + hp)
                for k in range(NT):
                    for hh in range(2):
                        v0 = HD * (2 * hp + hh)
                        pe.matmul(tp[2][HD * hh:HD * hh + HD, :], vB[:, k, v0:v0 + HD], pT[:, hh, k, :],
                                  start=(k == 0), stop=False, skip_group_check=True)
                for g in range(1, NG):
                    for c in range(NT):
                        for hh in range(2):
                            v0 = HD * (g * B_HPG + 2 * hp + hh)
                            cols = slice(P * c, P * c + P)
                            mm = pe.matmul(tp[2][HD * hh:HD * hh + HD, cols], vB[:, c, v0:v0 + HD],
                                           pT_dil[:, hh, g - 1, cols], start=False, stop=(g == NG - 1),
                                           skip_group_check=True)
                mm.then_inc(pv_done, 1)

            pe.wait_ge(a_turned_read, 3 * NT)
            scores_a(0)
            for u in range(NA):
                if u + 1 < NA:
                    scores_a(u + 1)
                if u and u % (2 * NT) == 0:
                    values_a(u // (2 * NT) - 1)
                turn_probs(u)
            values_a(OA - 1)
            pe.wait_ge(exp_done, NA)
            for hp in range(2):
                for kind in "qk":
                    for g in range(NG):
                        if hp and kind == "q" and g == 0:
                            pe.wait_ge(score_read, 2 * NT)
                        col_group(("col", kind, g, hp), at[(kind, g, hp)])
                pe.wait_ge(proj_read_dve, 2 * NG * (hp + 1))
                first, end = NA + 2 * NT * hp, NA + 2 * NT * (hp + 1)
                scores_b(first)
                for u in range(first, end):
                    if u + 1 < end:
                        scores_b(u + 1)
                    turn_probs(u)
                values_b(hp)

            pe.wait_ge(score_read, 4 * NT)
            for j in range(KC):
                col_group(("gate", j, 0), at[("ga", j)])
                col_group(("gate", j, 1), at[("gb", j)])
                n0 = at[("wo", j)]
                pe.wait_ge(w_split, n0 + 1)
                if j == 0:
                    pe.wait_ge(o_lo_done, OA + OB)
                if j >= 2:
                    pe.wait_ge(gates_used, 2 * (j - 1))
                for b, (k0, k1) in enumerate(((0, OA), (OA, OA + OB))):
                    for k in range(k0, k1):
                        mm = split_product(tp[2 * (j % 2) + b][:, :], k - k0, k1 - k0,
                                           [w[:, n0 % RING, k, :] for w in (w_hi, w_lo)],
                                           [t[:, k, :] for t in (oT_hi, oT_lo)])
                    mm.then_inc(branch_done, 1)

            pe.wait_ge(m_lo_done, KC)
            for p in range(D // P // 2):
                for c in range(NT):
                    tok_group(("res", p, c), at[("out", 2 * p)], (mT_hi, mT_lo))

            for c in range(NT):
                pe.wait_ge(xn_done, c + 1)
                for k in range(KC):
                    t = pe.transpose(bank[k][:, P * c:P * c + P], xn[:, c, P * k:P * k + P], ident[:, :])
                    if c == NT - 1:
                        t.then_inc(xn_turned, 1)
            pe.wait_ge(router_in, 16 * 3)
            for k in range(KC):
                pe.wait_ge(h2T_done, k + 1)
                mm = pe.matmul(bank[0][0:NE, :], w_rt[:, k, :], h2T[:, k, :], start=(k == 0), stop=(k == KC - 1))
            mm.then_inc(logits_done, 1)
            pe.wait_ge(h2T_done, KC)
            pe.wait_ge(logits_read, 1)
            for c in range(NT):
                t = pe.transpose(bank[1][:, NE * c:NE * c + NE], logitT[0:NE, P * c:P * c + P],
                                 ident[0:NE, 0:NE])
            t.then_inc(route_turned, 1)
            pe.wait_ge(aff_done, 1)
            for c in range(NT):
                t = pe.transpose(bank[2][0:NE, P * c:P * c + P], aff[:, c, :], ident[:, :])
            t.then_inc(route_turned, 1)
            pe.wait_ge(pos_done, 1)
            for c in range(NT):
                t = pe.transpose(bank[3][:, NE * c:NE * c + NE],
                                 count[0:NE, :].rearrange("e (i c) -> e c i", c=NT)[:, c, :], ident[0:NE, 0:NE])
            t.then_inc(route_turned, 1)

            with pe.Fori(0, NE // 4) as q:
                pe.wait_ge(pick_done, 2 * q + 1)
                for b in range(4):
                    if b >= 2:
                        pe.wait_ge(xin_done, 4 * q + (b - 1))
                    for j in range(2):
                        k = 2 * b + j
                        for c in range(NT):
                            for part in (xn_hi, xn_lo):
                                mm = pe.matmul(bank[4 + b % 2][:, 4 * CAP * j:4 * CAP * (j + 1)],
                                               part[:, c, P * k:P * k + P], pick[:, c, :, :],
                                               start=(c == 0 and part is xn_hi),
                                               stop=(c == NT - 1 and part is xn_lo))
                    mm.then_inc(gathered, 1)
                pe.wait_ge(pick_done, 2 * q + 2)
                pe.wait_ge(added, 16 * q + 1)
                for pr in range(2):
                    for c in range(NT):
                        t = pe.transpose(bank[6 + pr][:, P * c:P * c + P],
                                         pick_g[:, c, 2 * pr:2 * pr + 2, :].rearrange("p a s -> p (a s)"),
                                         ident[:, :])
                    t.then_inc(give_turned, 1)
                pe.wait_ge(xin_done, 4 * q + 4)
                for i in range(4):
                    for m in range(2):
                        for k in range(KC):
                            s = 2 * m + k // HALF
                            if k % HALF == 0:
                                pe.wait_ge(w_slot_in[s], 64 * q + 16 * (i + 1))
                            for f in range(2):
                                mm = pe.matmul(bank[m][CAP * f:CAP * f + CAP, :],
                                               xinT[:, k, CAP * i:CAP * i + CAP],
                                               wslot[s][:, k % HALF, SEQ * f:SEQ * f + SEQ],
                                               start=(k == 0), stop=(k == KC - 1))
                            if k % HALF == HALF - 1:
                                mm.then_inc(w_slot_used[s], 1)
                    pe.wait_ge(act_done, 4 * q + (i + 1))
                    for k in range(NT):
                        t = pe.transpose(bank[2][:, P * k:P * k + P], act[:, P * k:P * k + P], ident[:, :])
                    t.then_inc(act_turned, 1)
                    pe.wait_ge(actT_done, 4 * q + (i + 1))
                    if i:
                        pe.wait_ge(y_done, 4 * q + i)
                    for k in range(KC):
                        s, kk = 4 + k // HALF, k % HALF
                        if kk == 0:
                            pe.wait_ge(w_slot_in[s], 64 * q + 16 * (i + 1))
                        for f in range(2):
                            mm = pe.matmul(bank[3][CAP * f:CAP * f + CAP, :],
                                           actT[:, kk, CAP * (s - 4):CAP * (s - 4) + CAP],
                                           wslot[s][:, kk, SEQ * f:SEQ * f + SEQ],
                                           start=(k == 0), stop=(k == KC - 1))
                        if kk == HALF - 1:
                            mm.then_inc(w_slot_used[s], 1)
                    if i % 2:
                        pe.wait_ge(y_done, 4 * q + (i + 1))
                        pe.wait_ge(give_done, 2 * q + 2)
                        for n in range(8):
                            c, f = divmod(n, 2)
                            pe.wait_ge(added, 16 * q + (8 * (i // 2) + max(n - 1, 0) + 1))
                            pe.matmul(bank[6 + n % 2][:, :], give[:, i // 2, P * c:P * c + P],
                                      yE[:, SEQ * f:SEQ * f + SEQ], start=True, stop=True).then_inc(scattered, 1)

        @block.vector
        def _(dve):
            steps = [0]

            def settle(ins):
                ins.then_inc(dve_step, 1)
                steps[0] += 1
                dve.wait_ge(dve_step, steps[0])

            dve.wait_ge(consts_in, 16 * 7)
            for n, g in enumerate((gq, gk)):
                dve.tensor_tensor(rope_t[:, n, 0, :, :], rope_in[:, 0, :, :],
                                  g[:, :].unsqueeze(1).to_broadcast([P, NT, HD]), ALU.mult)
                g_b = g[:, :].rearrange("p (a b i) -> p a b i", a=2, b=2)
                for b in range(2):
                    dst = rope_t[:, n, 1, :, :].rearrange("p c (a b i) -> p c a b i", a=2, b=2)[:, :, :, b, :]
                    src = rope_in[:, 1, :, :].rearrange("p c (a b i) -> p c a b i", a=2, b=2)[:, :, :, b, :]
                    last = dve.tensor_tensor(dst, src, g_b[:, :, 1 - b, :].unsqueeze(1)
                                             .to_broadcast([P, NT, 2, HD // 4]), ALU.mult)
            settle(last)

            for c in range(NT):
                dve.wait_ge(rstd_done, c + 1)
                dve.tensor_scalar(x_in[:, c, :], x_in[:, c, :], rstd[:, c:c + 1], None, ALU.mult)\
                    .then_inc(x_normed, 1)
            for k in range(KC):
                dve.wait_ge(hT_hi_done, k + 1)
                dve.scalar_tensor_tensor(hT_lo[:, k, :], bank[k][:, :], g1[:, k:k + 1],
                                         hT_hi[:, k, :].bitcast(F32), ALU.mult, ALU.subtract)\
                    .then_inc(hT_lo_done, 1)

            NH = A_HEADS + A_KV
            dve.wait_ge(proj_read_act, 3 * NT)
            for c in range(NT):
                if c:
                    dve.wait_ge(a_sumsq, c)
                settle(dve.tensor_tensor(t1[:, :, :], zA[:, c], zA[:, c], ALU.mult))
                dve.tensor_reduce(ssqA[:, NH * c:NH * c + NH], t1[:, :, :], AX, ALU.add).then_inc(a_sumsq, 1)
            dve.wait_ge(a_sumsq, NT)
            for c in range(NT):
                dve.wait_ge(a_rstd, c + 1)
                settle(dve.tensor_tensor(zA[:, c], zA[:, c], rstdA[:, NH * c:NH * c + NH].unsqueeze(2)
                                         .to_broadcast([P, NH, HD]), ALU.mult))
                for n, h0, h1 in ((0, 0, A_HEADS), (1, A_HEADS, NH)):
                    nh = h1 - h0
                    dve.tensor_tensor(t1[:, h0:h1, :], zA[:, c, h0:h1, :],
                                      rope_t[:, n, 0, c, :].unsqueeze(1).to_broadcast([P, nh, HD]), ALU.mult)
                    z_b = zA[:, c, h0:h1, :].rearrange("p h (a b i) -> p h a b i", a=2, b=2)
                    t_b = t2[:, h0:h1, :].rearrange("p h (a b i) -> p h a b i", a=2, b=2)
                    s_b = rope_t[:, n, 1, c, :].rearrange("p (a b i) -> p a b i", a=2, b=2)
                    for b in range(2):
                        last = dve.tensor_tensor(t_b[:, :, :, b, :], z_b[:, :, :, 1 - b, :],
                                                 s_b[:, :, b, :].unsqueeze(1).to_broadcast([P, nh, 2, HD // 4]),
                                                 ALU.mult)
                settle(last)
                settle(dve.tensor_tensor(t1[:, :, :], t1[:, :, :], t2[:, :, :], ALU.add))
                if c >= 2:
                    dve.wait_ge(a_turned, 3 * (c - 1))
                q_hi, q_lo = q_parts[:, c % 2, :, 0, :], q_parts[:, c % 2, :, 1, :]
                k_p = k_parts[:, c % 2]
                dve.tensor_copy(q_hi, t1[:, 0:A_HEADS, :])
                dve.tensor_copy(k_p[:, :, 2, :], t1[:, A_HEADS:NH, :])
                settle(dve.tensor_copy(k_p[:, :, 0, :], t1[:, A_HEADS:NH, :]))
                dve.tensor_tensor(q_lo, t1[:, 0:A_HEADS, :], q_hi.bitcast(F32), ALU.subtract)
                dve.tensor_tensor(k_p[:, :, 1, :], t1[:, A_HEADS:NH, :], k_p[:, :, 0, :].bitcast(F32),
                                  ALU.subtract).then_inc(a_parts, 1)
                dve.wait_ge(a_parts, c + 1)

            def norm_probs(u, width):
                dve.wait_ge(exp_done, u + 1)
                settle(dve.reciprocal(rinv[:, u % 2:u % 2 + 1], rsum[:, u % 2:u % 2 + 1]))
                p = probs[:, u % 2, 0:width]
                dve.tensor_scalar(p, p, rinv[:, u % 2:u % 2 + 1], None, ALU.mult).then_inc(probs_normed, 1)

            def low_o(i):
                dve.wait_ge(o_hi_done, i + 1)
                dve.tensor_tensor(oT_lo[:, i, :], tp[2][:, :], oT_hi[:, i, :].bitcast(F32), ALU.subtract)\
                    .then_inc(o_lo_done, 1)

            for u in range(NA + 1):
                if u < NA:
                    dve.wait_ge(score_done, u + 1)
                    dve.tensor_reduce(nmax[:, u % 2:u % 2 + 1], pp[u % 2][:, :], AX, ALU.max, negate=True)\
                        .then_inc(nmax_done, 1)
                if u >= 1:
                    norm_probs(u - 1, SEQ)
                if u >= 10 and u % 8 == 2:
                    low_o(u // 8 - 1)
            low_o(OA - 1)

            dve.wait_ge(dist_in, 16)
            for hp in range(2):
                for kind in "qk":
                    for g in range(NG):
                        n = g_at[("col", kind, g, hp)]
                        dve.wait_ge(col_hi_done, n - N_TOK + 1)
                        src = pp[n % 4]
                        for hh in range(2):
                            half = slice(HD * hh, HD * hh + HD)
                            other = slice(HD - HD * hh, 2 * HD - HD * hh)
                            if kind == "q":
                                last = dve.scalar_tensor_tensor(
                                    qB[other, hh, g, :], src[half, :], SCALE,
                                    qB[half, hh, g, :].bitcast(F32), ALU.mult, ALU.subtract)
                            else:
                                hi = kB[half, hh, g, 0, :].bitcast(F32)
                                dve.tensor_tensor(kB[other, hh, g, 0, :], src[half, :], hi, ALU.subtract)
                                last = dve.tensor_tensor(kB[half, hh, g, 1, :], src[half, :], hi, ALU.subtract)
                        last.then_inc(proj_read_dve, 1)
                first, end = NA + 2 * NT * hp, NA + 2 * NT * (hp + 1)
                for u in range(first, end + 1):
                    if u < end:
                        head, c = divmod(u - NA, NT)
                        dve.wait_ge(score_done, u + 1)
                        dve.wait_ge(probs_turned, u - 1)
                        for g in range(NG):
                            src, far, dst = \
                                (pp[u % 2][:, :], dist[:, c, :], probs[:, u % 2, 0:SEQ]) if g == 0 else \
                                (pp[2 + u % 2][:, P * (g - 1):P * g], dist[:, NT, P * (g - 1):P * g],
                                 probs[:, u % 2, SEQ + P * (g - 1):SEQ + P * g])
                            last = dve.scalar_tensor_tensor(dst, far, -SLOPES[g * B_HPG + head], src,
                                                            ALU.mult, ALU.add)
                        last.then_inc(score_read, 1)
                        dve.wait_ge(score_read, u - NA + 1)
                        dve.tensor_reduce(nmax[:, u % 2:u % 2 + 1], probs[:, u % 2, :], AX, ALU.max,
                                          negate=True).then_inc(nmax_done, 1)
                    if u > first:
                        norm_probs(u - 1, SEQ + 2 * P)
                low_o(OA + hp)

            for j in range(KC):
                dve.wait_ge(proj_read_act, N_TOK + 2 * (j + 1))
                dve.wait_ge(branch_done, 2 * (j + 1))
                if j:
                    dve.wait_ge(m_hi_done, j)
                    dve.wait_ge(m_lo_done, j)
                for b, m in enumerate((m_a, m_b)):
                    dve.tensor_tensor(m[:, :], stage_e[:, b, :], tp[2 * (j % 2) + b][:, :], ALU.mult)\
                        .then_inc(gates_used, 1)
                dve.wait_ge(gates_used, 2 * (j + 1))
                dve.tensor_tensor(m_a[:, :], m_a[:, :], m_b[:, :], ALU.add).then_inc(merged, 1)
                dve.wait_ge(m_hi_done, j + 1)
                dve.tensor_tensor(mT_lo[:, j, :], m_a[:, :], mT_hi[:, j, :].bitcast(F32), ALU.subtract)\
                    .then_inc(m_lo_done, 1)

            dve.wait_ge(x_again_in, 16)
            for p in range(D // P // 2):
                for c in range(NT):
                    n = g_at[("res", p, c)]
                    dve.wait_ge(proj_done, n + 1)
                    part = x2[:, c, 2 * P * p:2 * P * (p + 1)]
                    dve.tensor_tensor(part, part, pp[n % 4][:, 0:2 * P], ALU.add).then_inc(proj_read_dve, 1)

            for c in range(NT):
                dve.wait_ge(rstd2, c + 1)
                dve.tensor_scalar(xn[:, c, :], x2[:, c, :], rstd[:, c:c + 1], None, ALU.mult)\
                    .then_inc(xn_done, 1)
            for c in range(NT):
                dve.wait_ge(xn_hi_done, c + 1)
                dve.tensor_tensor(xn_lo[:, c, :], xn[:, c, :], xn_hi[:, c, :].bitcast(F32), ALU.subtract)\
                    .then_inc(xn_lo_done, 1)

            dve.wait_ge(route_turned, 1)
            logits = bank[1][:, 0:NT * NE].rearrange("p (c e) -> p c e", e=NE)
            dve.tensor_reduce(smax, logits, AX, ALU.max, negate=True).then_inc(smax_done, 1)
            dve.wait_ge(sexp_done, NT)
            settle(dve.reciprocal(sinv, ssum))
            dve.tensor_tensor(aff[:, :, :], logit[:, :, :], sinv.unsqueeze(2).to_broadcast([P, NT, NE]),
                              ALU.mult).then_inc(aff_done, 1)

            dve.memset(zeros[0:NE, :], 0.0)
            dve.wait_ge(route_turned, 2)
            settle(dve.tensor_copy(affT[0:NE, :].rearrange("e (i c) -> e c i", c=NT),
                                   bank[2][0:NE, :].rearrange("e (c i) -> e c i", c=NT)))
            row = affT
            for r in range(CAP // 8):
                eight = best[0:NE, 8 * r:8 * r + 8]
                settle(dve.max(eight, row[0:NE, :] if r == 0 else row))
                nxt = left[0:NE, r % 2, :]
                settle(dve.match_replace(nxt, eight, row[0:NE, :] if r == 0 else row, -1.0))
                row = nxt
            settle(dve.tensor_scalar(taken[0:NE, :], row, 0.0, None, ALU.is_lt))
            settle(dve.tensor_tensor_scan(count[0:NE, :], taken[0:NE, :], zeros[0:NE, :], 0.0, ALU.add, ALU.add))
            settle(dve.tensor_tensor(count[0:NE, :], count[0:NE, :], taken[0:NE, :], ALU.mult))
            dve.tensor_scalar(count[0:NE, :], count[0:NE, :], -1.0, None, ALU.add).then_inc(pos_done, 1)
            dve.wait_ge(route_turned, 3)
            dve.tensor_copy(pos[:, :, :], bank[3][:, 0:NT * NE].rearrange("p (c e) -> p c e", e=NE))\
                .then_inc(added, 1)
            dve.wait_ge(added, 1)
            dve.wait_ge(xn_lo_done, NT)

            with dve.Fori(0, NE // 4) as q:
                wide = [P, NT, 4, CAP]
                place = slot_id[:, :].unsqueeze(1).unsqueeze(1).to_broadcast(wide)
                own = pos[:, :, bass.ds(4 * q, 4)].unsqueeze(3).to_broadcast(wide)
                dve.tensor_tensor(pick[:, :, :, :], place, own, ALU.is_equal).then_inc(pick_done, 1)
                dve.wait_ge(pick_done, 2 * q + 1)
                dve.tensor_tensor(pick_g[:, :, :, :], pick[:, :, :, :].bitcast(F32),
                                  aff[:, :, bass.ds(4 * q, 4)].unsqueeze(3).to_broadcast(wide), ALU.mult)\
                    .then_inc(pick_done, 1)
                for pr in range(2):
                    dve.wait_ge(give_turned, 2 * q + (pr + 1))
                    dve.tensor_copy(give[:, pr, :], bank[6 + pr][:, :]).then_inc(give_done, 1)
                for i in range(4):
                    dve.wait_ge(sig_done, 4 * q + (i + 1))
                    if i:
                        dve.wait_ge(act_turned, 4 * q + i)
                    dve.tensor_tensor(act[:, :], sig[:, :], bank[0][:, :], ALU.mult).then_inc(silu_half, 1)
                    dve.wait_ge(silu_half, 4 * q + (i + 1))
                    dve.wait_ge(w_slot_used[3], 4 * q + (i + 1))
                    dve.tensor_tensor(act[:, :], act[:, :], bank[1][:, :], ALU.mult).then_inc(act_done, 1)
                    if i % 2:
                        for n in range(8):
                            c, f = divmod(n, 2)
                            dve.wait_ge(scattered, 16 * q + (8 * (i // 2) + n + 1))
                            part = x2[:, c, SEQ * f:SEQ * f + SEQ]
                            dve.tensor_tensor(part, part, bank[6 + n % 2][:, :], ALU.add).then_inc(added, 1)

            for c in range(NT):
                dve.wait_ge(rstd3, c + 1)
                dve.scalar_tensor_tensor(fin[:, c, :], x2[:, c, :], rstd[:, c:c + 1], gf[:, :],
                                         ALU.mult, ALU.mult).then_inc(fin_done, 1)


_INS = ["x", "norm1_g", "w_in", "b_gates", "q_norm_g", "k_norm_g", "w_o_a", "w_o_b", "w_out", "norm2_g",
        "w_router", "w_gate", "w_up", "w_down", "normf_g"]


def shape_constants():
    f = np.float32
    token = NT * np.arange(P)[:, None] + np.arange(NT)[None, :]
    half = HD // 2
    inv_freq = f(1.0) / (f(ROPE_THETA) ** (np.arange(0, half, 2, dtype=f) / f(half)))
    rope = np.zeros((P, 2, NT, 2, 2, HD // 4), f)
    for a, coord in enumerate((token // GRID_W, token % GRID_W)):
        angle = coord.astype(f)[..., None] * inv_freq
        rope[:, 0, :, a, :, :] = np.cos(angle)[:, :, None, :]
        rope[:, 1, :, a, 0, :] = -np.sin(angle)
        rope[:, 1, :, a, 1, :] = np.sin(angle)
    distance = np.zeros((P, NT + 1, SEQ), f)
    i, j = np.arange(P)[:, None], np.arange(P)[None, :]
    for c in range(NT):
        for k in range(NT):
            far = np.abs(NT * (i - j) + c - k)
            distance[:, c, P * k:P * k + P] = np.where(far <= B_GROUPS[0][0] // 2, far, FAR)
    for g in (1, 2):
        window, dil = B_GROUPS[g]
        far = NT * np.abs(i - j)
        distance[:, NT, P * (g - 1):P * g] = np.where((far <= window // 2) & (far % dil == 0), far, FAR)
    slots = np.tile(np.arange(CAP, dtype=f), (P, 1))
    return {"identity": np.eye(P, dtype=f), "rope": rope.reshape(P, 2, NT, HD), "distance": distance,
            "slots": slots}


def kernel(**inputs):
    import concourse.bacc as _bacc
    from concourse.bass_utils import run_bass_kernel_spmd as _run

    nc = _bacc.Bacc("TRN2", target_bir_lowering=False, num_devices=1)
    given = {name: np.ascontiguousarray(inputs[name]) for name in _INS} | shape_constants()
    arrays, args = {}, {}
    for name, a in given.items():
        arrays[f"in_{name}"] = a
        args[name] = nc.dram_tensor(f"in_{name}", a.shape, mybir.dt.from_np(a.dtype), kind="ExternalInput").ap()
    out = nc.dram_tensor("out", (1, SEQ, D), F32, kind="ExternalOutput").ap()
    encoder_block(nc, out=out, **args)
    r = _run(nc, [arrays], core_ids=[0])
    return r.results[0]["out"]
```

```python
import math
from contextlib import ExitStack

import numpy as np

import concourse.bass as bass
from concourse import mybir

ALU = mybir.AluOpType
ACT = mybir.ActivationFunctionType
F32 = mybir.dt.float32
F32R = mybir.dt.float32r
AX = mybir.AxisListType.X

P = 128
SEQ = 512
D = 1024
NT = SEQ // P
KC = D // P
HD = 64
A_HEADS, A_KV = 8, 2
B_GROUPS = ((128, 1), (512, 4), (2048, 16))
NG = len(B_GROUPS)
B_HPG = 4
B_HEADS = NG * B_HPG
A_Q_W, A_KV_W, B_W = A_HEADS * HD, A_KV * HD, B_HEADS * HD
NE = 16
FF = 1024
CAP = 2 * SEQ // NE
EPS = 1e-6
GRID_W = 64
ROPE_THETA = 10000.0
FAR = 1e32
HUGE = 3e38
KIB = 1024

COL_A = 0
COL_BQ = A_Q_W + 2 * A_KV_W
COL_BK = COL_BQ + B_W
COL_BV = COL_BK + B_W
COL_GA = COL_BV + B_W
COL_GB = COL_GA + D
RING = 4
SLOTS = 8
SCALE = HD ** -0.5
SLOPES = [2.0 ** (-8.0 * (i + 1) / B_HEADS) for i in range(B_HEADS)]


def strips_in_order():
    out = [("a", i) for i in range((A_Q_W + 2 * A_KV_W) // P)]
    out += [("v", i) for i in range(B_W // P)]
    for hp in range(B_HPG // 2):
        out += [(kind, g, hp) for kind in "qk" for g in range(NG)]
    for j in range(KC):
        out += [("ga", j), ("gb", j), ("wo", j)]
    return out + [("out", i) for i in range(D // P)]


def encoder_block(nc, x, norm1_g, w_in, b_gates, q_norm_g, k_norm_g, w_o_a, w_o_b, w_out, norm2_g,
                  w_router, w_gate, w_up, w_down, normf_g, identity, rope, distance, slots, out):
    strips = strips_in_order()
    at = {s: n for n, s in enumerate(strips)}
    w_in_k = w_in[0].rearrange("(k p) n -> p k n", p=P)
    w_oa_k = w_o_a[0].rearrange("(k p) n -> p k n", p=P)
    w_ob_k = w_o_b[0].rearrange("(k p) n -> p k n", p=P)
    w_out_k = w_out[0].rearrange("(k p) n -> p k n", p=P)
    x_t = x[0].rearrange("(i c) d -> i c d", c=NT)
    out_t = out[0].rearrange("(i c) d -> i c d", c=NT)
    OA, OB = A_Q_W // P, B_HPG * HD // P

    base = (nc.sbuf_base + 31) // 32 * 32

    def sb(name, shape, kib, dt=F32):
        return nc.alloc_sbuf_tensor_at(name, [P] + shape, dt, offset=base + int(kib * KIB))

    hT_hi = sb("hT_hi", [KC, SEQ], 0, F32R)
    hT_lo = sb("hT_lo", [KC, SEQ], 16, F32R)
    w_raw = sb("w_raw", [RING, KC, P], 32)
    w_hi = sb("w_hi", [RING, KC, P], 48, F32R)
    w_lo = sb("w_lo", [RING, KC, P], 64, F32R)
    oT_hi = sb("oT_hi", [OA + OB, SEQ], 80, F32R)
    oT_lo = sb("oT_lo", [OA + OB, SEQ], 92, F32R)
    ident = sb("ident", [P], 104)
    small = sb("small", [256], 104.5)
    rope_t = sb("rope_t", [2, 2, NT, HD], 105.5)
    stage_e = sb("stage_e", [2, SEQ], 105.5)
    W0 = 111.5
    x_in = sb("x_in", [NT, D], W0)
    g1_row = sb("g1_row", [D], W0 + 24)
    rope_in = sb("rope_in", [2, NT, HD], W0 + 16)
    t1 = sb("t1", [A_HEADS + A_KV, HD], W0 + 18)
    t2 = sb("t2", [A_HEADS + A_KV, HD], W0 + 20.5)
    pT = sb("pT", [2, NT, SEQ], W0)
    pT_dil = sb("pT_dil", [2, 2, SEQ], W0 + 16)
    probs_a = [sb(f"probs_a{i}", [SEQ], W0 + 24 + 2 * i) for i in range(3)]
    probs_b = [sb(f"probs_b{i}", [SEQ + 2 * P], W0 + at_) for i, at_ in enumerate((24, 27, 92, -6))]
    dist = sb("dist", [NT, SEQ + 2 * P], W0 + 30)
    vB = sb("vB", [NT, B_W], W0 + 42)
    vA = sb("vA", [NT, A_KV_W], W0 + 54)
    zA = sb("zA", [NT, A_HEADS + A_KV, HD], W0 + 56)
    q_parts = sb("q_parts", [2, A_HEADS, 2, HD], W0, F32R)
    k_parts = sb("k_parts", [2, A_KV, 3, HD], W0 + 8, F32R)
    squares = sb("squares", [D], W0 + 54)
    qA = sb("qA", [A_HEADS, SEQ], W0 + 70, F32R)
    kA = sb("kA", [A_KV, 2, SEQ], W0 + 86, F32R)
    qB = sb("qB", [2, NG, SEQ], W0 + 56, F32R)
    kB = sb("kB", [2, NG, 2, SEQ], W0 + 68, F32R)
    m_a = sb("m_a", [SEQ], W0 + 48)
    m_b = sb("m_b", [SEQ], W0 + 50)
    mT_hi = sb("mT_hi", [KC, SEQ], W0 + 64, F32R)
    mT_lo = sb("mT_lo", [KC, SEQ], W0 + 80, F32R)
    x2 = sb("x2", [NT, D], 80)
    xn = sb("xn", [NT, D], 32)
    h2T = sb("h2T", [2, KC, P], 96)
    aff = sb("aff", [NT, NE], 109.5)
    pos = sb("pos", [NT, NE], 109.75)
    slot_id = sb("slot_id", [CAP], 110)
    logit = sb("logit", [NT, NE], 110.25)
    w_rt = sb("w_rt", [KC, NE], 110.5)
    affT = sb("affT", [SEQ], 62)
    left = sb("left", [2, SEQ], 64)
    taken = sb("taken", [SEQ], 68)
    count = sb("count", [SEQ], 70)
    zeros = sb("zeros", [SEQ], 72)
    best = sb("best", [CAP], 74)
    HALF = KC // 2
    wslot = [sb(f"wslot{i}", [HALF, D], kib) for i, kib in
             enumerate((W0, W0 + 16, W0 + 32, W0 + 48, 0, 16, W0 + 64, W0 + 80))]
    pick = sb("pick", [NT, 4, CAP], 48)
    pick_g = sb("pick_g", [NT, 4, CAP], 52)
    give = sb("give", [2, SEQ], 56)
    xinT = sb("xinT", [2, KC, 2 * CAP], 60)
    yE = sb("yE", [D], 68)
    act = sb("act", [SEQ], 72)
    sig = sb("sig", [SEQ], 74)
    actT = sb("actT", [NT, P], 76)
    gf = sb("gf", [D], 96)
    fin = sb("fin", [NT, D], 32)

    g2 = small[:, 8:16]
    bg = small[:, 16:32]
    ssq, rstd = small[:, 32:36], small[:, 36:40]
    neg_half = small[:, 40:80]
    ssqA, rstdA = small[:, 80:120], small[:, 120:160]
    nmax, rsum, rinv = small[:, 160:164], small[:, 164:168], small[:, 168:172]
    smax, ssum, sinv = small[:, 172:176], small[:, 176:180], small[:, 180:184]
    gq, gk = sb("gq", [HD], W0 + 95), sb("gk", [HD], W0 + 95.25)

    with ExitStack() as ctx:
        def sem(name):
            return ctx.enter_context(nc.semaphore(name))

        psum = ctx.enter_context(nc.psum_tensor("psum", [P, 8, 512], F32))
        bank = [psum[:, i, :] for i in range(8)]
        scores_two = [psum[:, 2 * i:2 * i + 2, :].rearrange("p b n -> p (b n)")[:, 0:SEQ + 2 * P]
                      for i in range(2)]
        turned_two = [psum[:, 4 + 2 * i:6 + 2 * i, :].rearrange("p b (k i) -> p (b k) i", i=P)
                      for i in range(2)]
        pp = bank[0:4]
        tp = bank[4:8]

        ident_in = sem("ident_in")
        g1_in = sem("g1_in")
        rope_parts_in = sem("rope_parts_in")
        gains_in = sem("gains_in")
        x_tile_in = [sem(f"x_tile_in{c}") for c in range(NT)]
        x_again_in = sem("x_again_in")
        dist_in = sem("dist_in")
        w_raw_in = [sem(f"w_raw_in{i}") for i in range(RING)]
        w_split = sem("w_split")
        w_hi_done = sem("w_hi_done")
        strip1_hi_done = sem("strip1_hi_done")
        strip1_split = sem("strip1_split")
        neg_half_set = sem("neg_half_set")
        sumsq_done = sem("sumsq_done")
        ms_done = sem("ms_done")
        rstd_done = sem("rstd_done")
        x_normed = sem("x_normed")
        x_turned = sem("x_turned")
        hT_hi_done = sem("hT_hi_done")
        hT_lo_done = sem("hT_lo_done")
        proj_done = sem("proj_done")
        proj_read_act = sem("proj_read_act")
        proj_read_dve = sem("proj_read_dve")
        dve_step = sem("dve_step")
        a_sumsq = sem("a_sumsq")
        a_ms = sem("a_ms")
        a_rstd = sem("a_rstd")
        a_parts = sem("a_parts")
        a_turned = sem("a_turned")
        a_turned_read = sem("a_turned_read")
        score_done = sem("score_done")
        nmax_done = sem("nmax_done")
        exp_done = sem("exp_done")
        probs_normed = sem("probs_normed")
        probs_turned = sem("probs_turned")
        pT_done = sem("pT_done")
        pv_done = sem("pv_done")
        o_hi_done = sem("o_hi_done")
        o_lo_done = sem("o_lo_done")
        col_hi_done = sem("col_hi_done")
        branch_done = sem("branch_done")
        gates_used = sem("gates_used")
        merged = sem("merged")
        silu_half = sem("silu_half")
        m_hi_done = sem("m_hi_done")
        m_lo_done = sem("m_lo_done")
        w_slot_in = [sem(f"w_slot_in{i}") for i in range(SLOTS)]
        w_slot_used = [sem(f"w_slot_used{i}") for i in range(SLOTS)]
        router_in = sem("router_in")
        gf_in = sem("gf_in")
        sumsq2 = sem("sumsq2")
        rstd2 = sem("rstd2")
        xn_done = sem("xn_done")
        xn_turned = sem("xn_turned")
        h2T_act_done = sem("h2T_act_done")
        h2T_dve_done = sem("h2T_dve_done")
        w_rt_scaled = sem("w_rt_scaled")
        logits_done = sem("logits_done")
        route_turned = sem("route_turned")
        smax_done = sem("smax_done")
        sexp_done = sem("sexp_done")
        aff_done = sem("aff_done")
        pos_done = sem("pos_done")
        pick_done = sem("pick_done")
        gathered = sem("gathered")
        xin_done = sem("xin_done")
        give_turned = sem("give_turned")
        give_done = sem("give_done")
        sig_done = sem("sig_done")
        act_done = sem("act_done")
        act_turned = sem("act_turned")
        actT_done = sem("actT_done")
        y_done = sem("y_done")
        scattered = sem("scattered")
        added = sem("added")
        ssq3 = sem("ssq3")
        rstd3 = sem("rstd3")
        fin_done = sem("fin_done")
        out_written = sem("out_written")

        groups = [("tok", kind, p, c) for kind in "av" for p in range(3) for c in range(NT)]
        groups += [("col",) + s for s in strips if s[0] in "qk"]
        groups += [("gate", j, b) for j in range(KC) for b in range(2)]
        groups += [("res", p, c) for p in (0, 1) for c in range(NT)]
        groups += [("res", p, c) for p, c in ((2, 0), (2, 1), (3, 0), (3, 1), (2, 2), (3, 2), (2, 3), (3, 3))]
        g_at = {g: n for n, g in enumerate(groups)}
        by_act = [g[0] in ("tok", "gate") for g in groups]

        NA = A_HEADS * NT
        N_RES = D // P // 2 * NT
        RES0 = g_at[("res", 0, 0)]
        N_COL = 2 * NG * 2
        N_TOK = 6 * NT

        def probs_of(u):
            return probs_a[u % 3] if u < NA else probs_b[u % 4]

        def wait_probs_free(eng, u):
            before = u - 3 if u < NA else max(u - 4, NA - 1)
            if before >= 0:
                eng.wait_ge(probs_turned, before + 1)

        def column(of, u):
            return of[:, u % 4:u % 4 + 1]

        def tile_summed(eng, c):
            eng.wait_ge(proj_read_dve, N_COL + g_at[("res", 3, c)] - RES0 + 1)

        def slot_of(i, j):
            return (6 * i + j) % SLOTS

        def slot_round(i, j):
            return (6 * i + j) // SLOTS + 1

        ROUNDS = 24 // SLOTS

        def wait_split(eng, n):
            if n == 1:
                eng.wait_ge(strip1_split, 1)
            else:
                eng.wait_ge(w_split, n + 1 if n == 0 else n)

        def wait_used(eng, n):
            kind, i = strips[n][0:2]
            if kind in "av":
                eng.wait_ge(proj_done, g_at[("tok", kind, i // 2, NT - 1)] + 1)
            elif kind in "qk":
                eng.wait_ge(proj_done, g_at[("col",) + strips[n]] + 1)
            elif kind == "wo":
                eng.wait_ge(branch_done, 2 * (i + 1))
            elif kind == "out":
                eng.wait_ge(proj_done, g_at[("res", i // 2, NT - 1)] + 1)
            else:
                eng.wait_ge(proj_done, g_at[("gate", i, int(kind == "gb"))] + 1)

        block = ctx.enter_context(nc.Block())

        @block.sync
        def _(sp):
            def load_x(c):
                sp.dma_start(x_in[:, c, :], x_t[:, c, :]).then_inc(x_tile_in[c], 16)

            def load_strip(n):
                s = strips[n]
                if n >= RING:
                    wait_split(sp, n - RING)
                raw = w_raw[:, n % RING]
                done = w_raw_in[n % RING]
                if s[0] == "wo":
                    cols = slice(P * s[1], P * (s[1] + 1))
                    sp.dma_start(raw[:, 0:OA, :], w_oa_k[:, :, cols]).then_inc(done, 16)
                    sp.dma_start(raw[:, OA:OA + OB, :], w_ob_k[:, :, cols]).then_inc(done, 16)
                    return
                if s[0] == "out":
                    sp.dma_start(raw, w_out_k[:, :, P * s[1]:P * (s[1] + 1)]).then_inc(done, 16)
                    return
                if s[0] == "q":
                    col = COL_BQ + (s[1] * B_HPG + 2 * s[2]) * HD
                elif s[0] == "k":
                    col = COL_BK + (s[1] * B_HPG + 2 * s[2]) * HD
                else:
                    col = {"a": COL_A, "v": COL_BV, "ga": COL_GA, "gb": COL_GB}[s[0]] + P * s[1]
                sp.dma_start(raw, w_in_k[:, :, col:col + P]).then_inc(done, 16)

            def load_slot(slot, half, e):
                rows = (w_gate, w_up, w_down)[half // 2][0, e]\
                    .rearrange("(h k p) n -> h p k n", h=2, p=P)[half % 2]
                sp.dma_start(wslot[slot][:, :, :], rows).then_inc(w_slot_in[slot], 16)

            load_x(0)
            for n in range(len(strips)):
                load_strip(n)
                if n == 1:
                    for c in range(1, NT):
                        load_x(c)
                if strips[n] == ("gb", 1):
                    sp.wait_ge(pv_done, OA + OB)
                    for i in range(3):
                        load_slot(i, i, 0)
                if strips[n] == ("out", 3):
                    sp.wait_ge(branch_done, 2 * KC)
                    sp.dma_start(x2[:, :, :], x_t).then_inc(x_again_in, 16)
                    sp.wait_ge(proj_done, g_at[("gate", KC - 1, 1)] + 1)
                    load_slot(4, 4, 0)
                if strips[n] == ("out", 5):
                    load_slot(5, 5, 0)
            sp.wait_ge(m_hi_done, KC)
            sp.wait_ge(m_lo_done, KC)
            load_slot(3, 3, 0)
            sp.wait_ge(proj_done, len(groups))
            for i in (6, 7):
                load_slot(i, i - 6, 1)

            def load_again(q, m):
                sp.wait_ge(w_slot_used[m % SLOTS], ROUNDS * q + m // SLOTS)
                load_slot(m % SLOTS, m % 6, 4 * q + m // 6)

            with sp.Fori(0, NE // 4 - 1) as q:
                for m in range(SLOTS, 24 + SLOTS):
                    load_again(q, m)
            for m in range(SLOTS, 24):
                load_again(NE // 4 - 1, m)
            for c in range(NT):
                sp.wait_ge(fin_done, c + 1)
                sp.dma_start(out_t[:, c, :], fin[:, c, :]).then_inc(out_written, 16)
            sp.wait_ge(out_written, 16 * NT)

        @block.gpsimd
        def _(pool):
            pool.memset(neg_half, -0.5).then_inc(neg_half_set, 1)
            pool.wait_ge(neg_half_set, 1)

            def power(sums, into, n, width, counted, done, first):
                pool.tensor_scalar(into, sums, 1.0 / width, EPS, ALU.mult, ALU.add).then_inc(counted, 1)
                pool.wait_ge(counted, first + 1)
                pool.tensor_tensor(into, into, neg_half[:, 0:n], ALU.pow).then_inc(done, 1)

            def rstd_of_x(c):
                pool.wait_ge(sumsq_done, c + 1)
                power(ssq[:, c:c + 1], rstd[:, c:c + 1], 1, D, ms_done, rstd_done, c)

            def split_hi(n):
                arrived = sum(2 if t[0] == "wo" else 1 for t in strips[n % RING:n + 1:RING])
                pool.wait_ge(w_raw_in[n % RING], 16 * arrived)
                if n >= RING:
                    wait_used(pool, n - RING)
                k = OA + OB if strips[n][0] == "wo" else KC
                raw, hi = (w[:, n % RING, 0:k, :] for w in (w_raw, w_hi))
                pool.tensor_scalar(hi, raw, 1.0, 1.0, ALU.mult, ALU.mult).then_inc(w_hi_done, 1)

            def split_lo(n):
                pool.wait_ge(w_hi_done, n + 1 if n == 0 else n)
                k = OA + OB if strips[n][0] == "wo" else KC
                raw, hi, lo = (w[:, n % RING, 0:k, :] for w in (w_raw, w_hi, w_lo))
                pool.tensor_tensor(lo, raw, hi.bitcast(F32), ALU.subtract).then_inc(w_split, 1)

            split_hi(0)
            rstd_of_x(0)
            split_lo(0)
            for c in range(1, NT):
                rstd_of_x(c)
            for n in range(2, len(strips)):
                if n == at[("v", 4)]:
                    w = A_HEADS + A_KV
                    for c in range(NT):
                        pool.wait_ge(a_sumsq, c + 1)
                        power(ssqA[:, w * c:w * c + w], rstdA[:, w * c:w * c + w], w, HD, a_ms, a_rstd, c)
                split_hi(n)
                split_lo(n)

            for c in range(NT):
                pool.wait_ge(sumsq2, c + 1)
                power(ssq[:, c:c + 1], rstd[:, c:c + 1], 1, D, ms_done, rstd2, NT + c)
            for c in range(NT):
                pool.wait_ge(ssq3, c + 1)
                power(ssq[:, c:c + 1], rstd[:, c:c + 1], 1, D, ms_done, rstd3, 2 * NT + c)

        @block.scalar
        def _(act_):
            act_.dma_start(ident[:, :], identity).then_inc(ident_in, 16)
            act_.dma_start(g1_row[:, :], norm1_g[0].partition_broadcast(P)).then_inc(g1_in, 16)

            def square_x(c):
                act_.wait_ge(x_tile_in[c], 16)
                if c:
                    act_.wait_ge(sumsq_done, c)
                act_.activation(squares[:, :], x_in[:, c, :], ACT.Square,
                                accum_out=ssq[:, c:c + 1]).then_inc(sumsq_done, 1)

            def high_hT(c):
                act_.wait_ge(x_turned, c + 1)
                act_.activation(hT_hi[:, :, P * c:P * c + P], turned_two[c % 2], ACT.Copy).then_inc(hT_hi_done, 1)

            square_x(0)
            act_.dma_start(rope_in[:, :, :, :], rope).then_inc(rope_parts_in, 16)
            for dst, src in ((gq, q_norm_g), (gk, k_norm_g)):
                act_.dma_start(dst[:, :], src[0].partition_broadcast(P)).then_inc(rope_parts_in, 16)
            square_x(1)
            for c in range(2, NT):
                square_x(c)
                high_hT(c - 2)
            high_hT(NT - 2)
            high_hT(NT - 1)
            act_.dma_start(dist[:, :, :], distance).then_inc(dist_in, 16)
            for dst, src in ((g2, norm2_g[0]), (bg, b_gates[0])):
                act_.dma_start(dst, src.rearrange("(k p) -> p k", p=P),
                               allow_slow_non_contiguous=True).then_inc(gains_in, 16)
            act_.dma_start(w_rt[:, :, :], w_router[0].rearrange("(k p) e -> p k e", p=P)).then_inc(router_in, 16)
            act_.dma_start(slot_id[:, :], slots).then_inc(router_in, 16)

            def read_tok(kind, p, c):
                n = g_at[("tok", kind, p, c)]
                src = pp[n % 4][:, 0:2 * P]
                act_.wait_ge(proj_done, n + 1)
                if kind == "v":
                    act_.activation(vB[:, c, 2 * P * p:2 * P * (p + 1)], src, ACT.Copy)\
                        .then_inc(proj_read_act, 1)
                elif p < 2:
                    act_.activation(zA[:, c, 4 * p:4 * p + 4, :], src.rearrange("p (h d) -> p h d", d=HD),
                                    ACT.Copy).then_inc(proj_read_act, 1)
                else:
                    act_.activation(zA[:, c, 8:10, :], src[:, 0:P].rearrange("p (h d) -> p h d", d=HD), ACT.Copy)
                    act_.activation(vA[:, c, :], src[:, P:2 * P], ACT.Copy).then_inc(proj_read_act, 1)

            def read_turned(c):
                for b in range(3):
                    n = 3 * c + b
                    act_.wait_ge(a_turned, n + 1)
                    src = tp[n % 4][:, :].rearrange("p (h i) -> p h i", i=P)
                    cols = slice(P * c, P * c + P)
                    if b < 2:
                        act_.activation(qA[:, 4 * b:4 * b + 4, cols], src, ACT.Copy, scale=SCALE)\
                            .then_inc(a_turned_read, 1)
                    else:
                        dst = kA[:, :, :, cols].rearrange("p k v i -> p (k v) i")
                        act_.activation(dst, src, ACT.Copy).then_inc(a_turned_read, 1)

            for kind, p in (("a", 0), ("a", 1), ("a", 2), ("v", 0), ("v", 1)):
                for c in range(NT):
                    read_tok(kind, p, c)
            read_turned(0)
            read_tok("v", 2, 0)
            read_tok("v", 2, 1)
            read_turned(1)
            read_tok("v", 2, 2)
            read_tok("v", 2, 3)
            read_turned(2)
            read_turned(3)

            def soft_exp(u, width, src):
                act_.wait_ge(nmax_done, u + 1)
                wait_probs_free(act_, u)
                act_.activation(probs_of(u)[:, 0:width], src, ACT.Exp, bias=column(nmax, u),
                                scale=1.0 if u < NA else -1.0,
                                accum_out=column(rsum, u)).then_inc(exp_done, 1)

            def read_probs(u):
                head, c = divmod(u, NT)
                cols = slice(P * c, P * c + P)
                if head >= 2:
                    act_.wait_ge(pv_done, head // 2)
                act_.wait_ge(probs_turned, u + 1)
                last = act_.activation(pT[:, head % 2, :, cols],
                                       tp[(0, 3)[u % 2]][:, :].rearrange("p (k i) -> p k i", i=P), ACT.Copy)
                if u >= NA:
                    last = act_.activation(pT_dil[:, head % 2, :, cols],
                                           tp[1][:, 0:2 * P].rearrange("p (g i) -> p g i", i=P), ACT.Copy)
                last.then_inc(pT_done, 1)

            def read_o(i):
                act_.wait_ge(pv_done, i + 1)
                act_.activation(oT_hi[:, i, :], tp[2][:, :], ACT.Copy).then_inc(o_hi_done, 1)

            for u in range(NA + 2):
                if u < NA:
                    soft_exp(u, SEQ, pp[u % 4][:, :])
                if u >= 2:
                    read_probs(u - 2)
                if u >= 10 and u % 8 == 2 and u < NA:
                    read_o(u // 8 - 1)
            read_o(OA - 1)

            for hp in range(2):
                for kind in "qk":
                    for g in range(NG):
                        n = g_at[("col", kind, g, hp)]
                        act_.wait_ge(proj_done, n + 1)
                        src = pp[n % 4]
                        for hh in range(2):
                            half = slice(HD * hh, HD * hh + HD)
                            other = slice(HD - HD * hh, 2 * HD - HD * hh)
                            if kind == "q":
                                last = act_.activation(qB[half, hh, g, :], src[half, :], ACT.Copy,
                                                       scale=SCALE / SLOPES[2 * hp + hh])
                            else:
                                act_.activation(kB[half, hh, g, 0, :], src[half, :], ACT.Copy)
                                last = act_.activation(kB[other, hh, g, 1, :], src[half, :], ACT.Copy)
                        last.then_inc(col_hi_done, 1)
                first, end = NA + 2 * NT * hp, NA + 2 * NT * (hp + 1)
                for u in range(first, end + 2):
                    if u < end:
                        soft_exp(u, SEQ + 2 * P, probs_of(u)[:, :])
                    if u >= first + 2:
                        read_probs(u - 2)
                read_o(OA + hp)

            act_.wait_ge(gains_in, 16 * 2)
            for j in range(KC):
                for b in range(2):
                    n = g_at[("gate", j, b)]
                    act_.wait_ge(proj_done, n + 1)
                    if j:
                        act_.wait_ge(gates_used, 2 * j)
                    act_.activation(stage_e[:, b, :], pp[n % 4][:, :], ACT.Sigmoid,
                                    bias=bg[:, KC * b + j:KC * b + j + 1]).then_inc(proj_read_act, 1)
                act_.wait_ge(merged, j + 1)
                act_.activation(mT_hi[:, j, :], m_a[:, :], ACT.Copy).then_inc(m_hi_done, 1)

            def square_x2(c):
                tile_summed(act_, c)
                act_.activation(xn[:, c, :], x2[:, c, :], ACT.Square,
                                accum_out=ssq[:, c:c + 1]).then_inc(sumsq2, 1)

            def read_h2(c):
                act_.wait_ge(xn_turned, c + 1)
                if c >= 2:
                    act_.wait_ge(logits_done, c - 1)
                act_.activation(h2T[:, c % 2, 0:HALF, :],
                                tp[2 * (c % 2)][:, :].rearrange("p (k i) -> p k i", i=P), ACT.Copy)\
                    .then_inc(h2T_act_done, 1)

            def route_exp(c):
                act_.wait_ge(smax_done, c + 1)
                act_.activation(logit[:, c, :], bank[c][:, 0:NE], ACT.Exp,
                                bias=smax[:, c:c + 1], accum_out=ssum[:, c:c + 1]).then_inc(sexp_done, 1)

            for step, c in ((square_x2, 0), (square_x2, 1), (read_h2, 0), (square_x2, 2), (read_h2, 1),
                            (route_exp, 0), (read_h2, 2), (route_exp, 1), (square_x2, 3), (route_exp, 2),
                            (read_h2, 3), (route_exp, 3)):
                step(c)
            act_.wait_ge(logits_done, NT)
            act_.dma_start(gf[:, :], normf_g.partition_broadcast(P)).then_inc(gf_in, 16)

            with act_.Fori(0, NE // 4) as q:
                def read_gathered(pr, b):
                    act_.wait_ge(gathered, 4 * q + (2 * pr + b + 1))
                    for k in range(HALF):
                        last = act_.activation(xinT[:, pr, HALF * b + k, :], bank[4 + b][:, P * k:P * k + P],
                                               ACT.Copy, scale=g2[:, HALF * b + k:HALF * b + k + 1])
                    last.then_inc(xin_done, 1)

                read_gathered(0, 0)
                read_gathered(0, 1)
                for i in range(4):
                    act_.wait_ge(w_slot_used[slot_of(i, 1)], ROUNDS * q + slot_round(i, 1))
                    if i:
                        act_.wait_ge(act_done, 4 * q + i)
                    act_.activation(sig[:, :], bank[0][:, :], ACT.Sigmoid).then_inc(sig_done, 1)
                    if i == 1:
                        read_gathered(1, 0)
                        read_gathered(1, 1)
                    act_.wait_ge(act_turned, 4 * q + (i + 1))
                    act_.activation(actT[:, :, :], bank[2][:, :].rearrange("p (k i) -> p k i", i=P), ACT.Copy)\
                        .then_inc(actT_done, 1)
                    act_.wait_ge(w_slot_used[slot_of(i, 5)], ROUNDS * q + slot_round(i, 5))
                    rows = slice(CAP * (i % 2), CAP * (i % 2) + CAP)
                    act_.activation(yE[rows, 0:SEQ], bank[3][0:CAP, :], ACT.Copy)
                    act_.activation(yE[rows, SEQ:D], bank[3][CAP:2 * CAP, :], ACT.Copy).then_inc(y_done, 1)
                    if i % 2:
                        act_.wait_ge(scattered, 16 * q + 8 * (i // 2 + 1))

            for c in range(NT):
                act_.wait_ge(added, NE // 2 * 8 - 8 + 2 * (c + 1) + 1)
                act_.activation(fin[:, c, :], x2[:, c, :], ACT.Square,
                                accum_out=ssq[:, c:c + 1]).then_inc(ssq3, 1)

        @block.tensor
        def _(pe):
            def split_product(out_, k, n_k, stat, mov):
                (s_hi, s_lo), (m_hi, m_lo) = stat, mov
                pe.matmul(out_, s_hi, m_hi, start=(k == 0), stop=False)
                pe.matmul(out_, s_hi, m_lo, start=False, stop=False)
                return pe.matmul(out_, s_lo, m_hi, start=False, stop=(k == n_k - 1))

            def turn_x(c):
                pe.wait_ge(x_normed, c + 1)
                if c >= 2:
                    pe.wait_ge(hT_lo_done, c - 1)
                for k in range(KC):
                    t = pe.transpose(turned_two[c % 2][:, k, :], x_in[:, c, P * k:P * k + P], ident[:, :])
                t.then_inc(x_turned, 1)

            def pp_take(n):
                if n >= 4:
                    m = n - 4
                    if by_act[m]:
                        pe.wait_ge(proj_read_act, sum(by_act[:m + 1]))
                    else:
                        pe.wait_ge(proj_read_dve, m + 1 - sum(by_act[:m + 1]))

            def tok_group(group, n0, act_parts, parts_done=None):
                n, c = g_at[group], group[-1]
                wait_split(pe, n0)
                wait_split(pe, n0 + 1)
                pp_take(n)
                s = n0 % RING
                cols = slice(P * c, P * c + P)
                for k in range(KC):
                    if parts_done is not None:
                        pe.wait_ge(parts_done, k + 1)
                    mm = split_product(pp[n % 4][:, 0:2 * P], k, KC, [t[:, k, cols] for t in act_parts],
                                       [w[:, s:s + 2, k, :] for w in (w_hi, w_lo)])
                mm.then_inc(proj_done, 1)

            def col_group(group, n0):
                n = g_at[group]
                wait_split(pe, n0)
                pp_take(n)
                for k in range(KC):
                    mm = split_product(pp[n % 4][:, :], k, KC, [w[:, n0 % RING, k, :] for w in (w_hi, w_lo)],
                                       [t[:, k, :] for t in (hT_hi, hT_lo)])
                mm.then_inc(proj_done, 1)

            def turn_a(c):
                pe.wait_ge(a_parts, c + 1)
                for b in range(3):
                    n = 3 * c + b
                    if n >= 4:
                        pe.wait_ge(a_turned_read, n - 3)
                    for i in range(4):
                        src = q_parts[:, c % 2, 4 * b + i, :, :] if b < 2 else \
                            k_parts[:, c % 2, i // 2, i % 2:i % 2 + 2, :]
                        t = pe.transpose(tp[n % 4][:, P * i:P * i + P],
                                         src.rearrange("p a d -> p (a d)").bitcast(F32), ident[:, :])
                    t.then_inc(a_turned, 1)

            hT = (hT_hi, hT_lo)
            pe.wait_ge(ident_in, 16)
            turn_x(0)
            for c in range(NT):
                if c + 1 < NT:
                    turn_x(c + 1)
                pe.wait_ge(hT_lo_done, c + 1)
                tok_group(("tok", "a", 0, c), at[("a", 0)], hT)
            for kind, p in (("a", 1), ("a", 2), ("v", 0), ("v", 1)):
                for c in range(NT):
                    tok_group(("tok", kind, p, c), at[(kind, 2 * p)], hT)
            turn_a(0)
            tok_group(("tok", "v", 2, 0), at[("v", 4)], hT)
            tok_group(("tok", "v", 2, 1), at[("v", 4)], hT)
            turn_a(1)
            tok_group(("tok", "v", 2, 2), at[("v", 4)], hT)
            tok_group(("tok", "v", 2, 3), at[("v", 4)], hT)
            turn_a(2)
            turn_a(3)

            def scores_a(u):
                h, c = divmod(u, NT)
                if u >= 4:
                    pe.wait_ge(exp_done, u - 3)
                for v in range(2):
                    mm = pe.matmul(pp[u % 4][:, :], qA[:, h, P * c:P * c + P],
                                   kA[:, h // (A_HEADS // A_KV), v, :], start=(v == 0), stop=(v == 1))
                mm.then_inc(score_done, 1)

            def scores_b(u):
                head, c = divmod(u - NA, NT)
                cols = slice(P * c, P * c + P)
                if u >= NA + 2:
                    pe.wait_ge(nmax_done, u - 1)
                for g in range(NG):
                    dst = scores_two[u % 2][:, 0:SEQ] if g == 0 else \
                        scores_two[u % 2][:, SEQ + P * (g - 1):SEQ + P * g]
                    for v in range(2):
                        keys = kB[:, head % 2, g, v, :] if g == 0 else kB[:, head % 2, g, v, cols]
                        mm = pe.matmul(dst, qB[:, head % 2, g, cols], keys, start=(v == 0), stop=(v == 1))
                mm.then_inc(score_done, 1)

            def turn_probs(u):
                pe.wait_ge(probs_normed, u + 1)
                if u >= NA:
                    pe.wait_ge(pT_done, u)
                    for g in range(2):
                        pe.transpose(tp[1][:, P * g:P * g + P],
                                     probs_of(u)[:, SEQ + P * g:SEQ + P * g + P], ident[:, :])
                elif u >= 2:
                    pe.wait_ge(pT_done, u - 1)
                for k in range(NT):
                    t = pe.transpose(tp[(0, 3)[u % 2]][:, P * k:P * k + P],
                                     probs_of(u)[:, P * k:P * k + P], ident[:, :])
                t.then_inc(probs_turned, 1)

            def values_a(i):
                pe.wait_ge(pT_done, 2 * NT * (i + 1))
                if i:
                    pe.wait_ge(o_lo_done, i)
                kv = 2 * i // (A_HEADS // A_KV)
                for k in range(NT):
                    for hh in range(2):
                        mm = pe.matmul(tp[2][HD * hh:HD * hh + HD, :], vA[:, k, HD * kv:HD * kv + HD],
                                       pT[:, hh, k, :], start=(k == 0), stop=(k == NT - 1))
                mm.then_inc(pv_done, 1)

            def values_b(hp):
                pe.wait_ge(pT_done, NA + 2 * NT * (hp + 1))
                pe.wait_ge(o_lo_done, OA + hp)
                for k in range(NT):
                    for hh in range(2):
                        v0 = HD * (2 * hp + hh)
                        pe.matmul(tp[2][HD * hh:HD * hh + HD, :], vB[:, k, v0:v0 + HD], pT[:, hh, k, :],
                                  start=(k == 0), stop=False, skip_group_check=True)
                for g in range(1, NG):
                    for c in range(NT):
                        for hh in range(2):
                            v0 = HD * (g * B_HPG + 2 * hp + hh)
                            cols = slice(P * c, P * c + P)
                            mm = pe.matmul(tp[2][HD * hh:HD * hh + HD, cols], vB[:, c, v0:v0 + HD],
                                           pT_dil[:, hh, g - 1, cols], start=False, stop=(g == NG - 1),
                                           skip_group_check=True)
                mm.then_inc(pv_done, 1)

            pe.wait_ge(a_turned_read, 3 * NT)
            scores_a(0)
            scores_a(1)
            for u in range(NA):
                if u + 2 < NA:
                    scores_a(u + 2)
                if u > 1 and u % (2 * NT) == 1:
                    values_a(u // (2 * NT) - 1)
                turn_probs(u)
            values_a(OA - 1)
            pe.wait_ge(exp_done, NA)
            for hp in range(2):
                for kind in "qk":
                    for g in range(NG):
                        if hp and kind == "q" and g == 0:
                            pe.wait_ge(nmax_done, NA + 2 * NT)
                        col_group(("col", kind, g, hp), at[(kind, g, hp)])
                pe.wait_ge(proj_read_dve, 2 * NG * (hp + 1))
                first, end = NA + 2 * NT * hp, NA + 2 * NT * (hp + 1)
                scores_b(first)
                scores_b(first + 1)
                for u in range(first, end):
                    if u + 2 < end:
                        scores_b(u + 2)
                    turn_probs(u)
                values_b(hp)

            pe.wait_ge(nmax_done, NA + 4 * NT)
            for j in range(KC):
                col_group(("gate", j, 0), at[("ga", j)])
                col_group(("gate", j, 1), at[("gb", j)])
                n0 = at[("wo", j)]
                wait_split(pe, n0)
                if j == 0:
                    pe.wait_ge(o_lo_done, OA + OB)
                if j >= 2:
                    pe.wait_ge(gates_used, 2 * (j - 1))
                for b, (k0, k1) in enumerate(((0, OA), (OA, OA + OB))):
                    for k in range(k0, k1):
                        mm = split_product(tp[2 * (j % 2) + b][:, :], k - k0, k1 - k0,
                                           [w[:, n0 % RING, k, :] for w in (w_hi, w_lo)],
                                           [t[:, k, :] for t in (oT_hi, oT_lo)])
                    mm.then_inc(branch_done, 1)

            def turn_x2(c):
                pe.wait_ge(xn_done, c + 1)
                if c >= 2:
                    pe.wait_ge(h2T_act_done, c - 1)
                    pe.wait_ge(h2T_dve_done, c - 1)
                for k in range(KC):
                    t = pe.transpose(tp[2 * (c % 2) + k // HALF][:, P * (k % HALF):P * (k % HALF) + P],
                                     xn[:, c, P * k:P * k + P], ident[:, :])
                t.then_inc(xn_turned, 1)

            def route(c):
                pe.wait_ge(h2T_act_done, c + 1)
                pe.wait_ge(h2T_dve_done, c + 1)
                pe.wait_ge(proj_read_dve, N_COL + N_RES - NT + c + 1)
                for k in range(KC):
                    mm = pe.matmul(bank[c][:, 0:NE], h2T[:, c % 2, k, :], w_rt[:, k, :],
                                   start=(k == 0), stop=(k == KC - 1))
                mm.then_inc(logits_done, 1)

            def project(p, c):
                tok_group(("res", p, c), at[("out", 2 * p)], (mT_hi, mT_lo))

            tok_group(groups[RES0], at[("out", 0)], (mT_hi, mT_lo), m_lo_done)
            for group in groups[RES0 + 1:RES0 + 13]:
                project(*group[1:])
            pe.wait_ge(w_rt_scaled, 1)
            turn_x2(0)
            project(3, 2)
            turn_x2(1)
            route(0)
            project(2, 3)
            turn_x2(2)
            route(1)
            project(3, 3)
            route(2)
            turn_x2(3)
            route(3)
            pe.wait_ge(aff_done, NT)
            for c in range(NT):
                t = pe.transpose(bank[0][0:NE, P * c:P * c + P], aff[:, c, :], ident[:, :])
            t.then_inc(route_turned, 1)
            pe.wait_ge(pos_done, 1)
            for c in range(NT):
                t = pe.transpose(bank[1][:, NE * c:NE * c + NE],
                                 count[0:NE, :].rearrange("e (i c) -> e c i", c=NT)[:, c, :], ident[0:NE, 0:NE])
            t.then_inc(route_turned, 1)

            with pe.Fori(0, NE // 4) as q:
                def gather(pr):
                    pe.wait_ge(pick_done, 3 * q + (pr + 1))
                    for b in range(2):
                        if pr:
                            pe.wait_ge(xin_done, 4 * q + (b + 1))
                        for k in range(HALF):
                            for c in range(NT):
                                mm = pe.matmul(bank[4 + b][:, P * k:P * k + P],
                                               xn[:, c, P * (HALF * b + k):P * (HALF * b + k) + P],
                                               pick[:, c, 2 * pr:2 * pr + 2, :],
                                               start=(c == 0), stop=(c == NT - 1))
                        mm.then_inc(gathered, 1)

                gather(0)
                pe.wait_ge(pick_done, 3 * q + 3)
                pe.wait_ge(added, 16 * q + 1)
                for pr in range(2):
                    for c in range(NT):
                        t = pe.transpose(bank[6 + pr][:, P * c:P * c + P],
                                         pick_g[:, c, 2 * pr:2 * pr + 2, :].rearrange("p a s -> p (a s)"),
                                         ident[:, :])
                    t.then_inc(give_turned, 1)
                for i in range(4):
                    if i % 2 == 0:
                        pe.wait_ge(xin_done, 4 * q + (i + 2))
                    for m in range(2):
                        for k in range(KC):
                            half = 2 * m + k // HALF
                            s = slot_of(i, half)
                            if k % HALF == 0:
                                pe.wait_ge(w_slot_in[s], 16 * ROUNDS * q + 16 * slot_round(i, half))
                            for f in range(2):
                                mm = pe.matmul(bank[m][CAP * f:CAP * f + CAP, :],
                                               xinT[:, i // 2, k, CAP * (i % 2):CAP * (i % 2) + CAP],
                                               wslot[s][:, k % HALF, SEQ * f:SEQ * f + SEQ],
                                               start=(k == 0), stop=(k == KC - 1))
                            if k % HALF == HALF - 1:
                                mm.then_inc(w_slot_used[s], 1)
                    if i == 1:
                        gather(1)
                    pe.wait_ge(act_done, 4 * q + (i + 1))
                    for k in range(NT):
                        t = pe.transpose(bank[2][:, P * k:P * k + P], act[:, P * k:P * k + P], ident[:, :])
                    t.then_inc(act_turned, 1)
                    pe.wait_ge(actT_done, 4 * q + (i + 1))
                    if i:
                        pe.wait_ge(y_done, 4 * q + i)
                    for k in range(KC):
                        half, kk = 4 + k // HALF, k % HALF
                        s = slot_of(i, half)
                        if kk == 0:
                            pe.wait_ge(w_slot_in[s], 16 * ROUNDS * q + 16 * slot_round(i, half))
                        for f in range(2):
                            mm = pe.matmul(bank[3][CAP * f:CAP * f + CAP, :],
                                           actT[:, kk, CAP * (k // HALF):CAP * (k // HALF) + CAP],
                                           wslot[s][:, kk, SEQ * f:SEQ * f + SEQ],
                                           start=(k == 0), stop=(k == KC - 1))
                        if kk == HALF - 1:
                            mm.then_inc(w_slot_used[s], 1)
                    if i % 2:
                        pe.wait_ge(y_done, 4 * q + (i + 1))
                        pe.wait_ge(give_done, 2 * q + 2)
                        for n in range(8):
                            c, f = divmod(n, 2)
                            pe.wait_ge(added, 16 * q + (8 * (i // 2) + max(n - 1, 0) + 1))
                            pe.matmul(bank[6 + n % 2][:, :], give[:, i // 2, P * c:P * c + P],
                                      yE[:, SEQ * f:SEQ * f + SEQ], start=True, stop=True).then_inc(scattered, 1)

        @block.vector
        def _(dve):
            steps = [0]

            def settle(ins):
                ins.then_inc(dve_step, 1)
                steps[0] += 1
                dve.wait_ge(dve_step, steps[0])

            dve.wait_ge(g1_in, 16)

            def norm_x(c):
                dve.wait_ge(rstd_done, c + 1)
                dve.scalar_tensor_tensor(x_in[:, c, :], x_in[:, c, :], rstd[:, c:c + 1], g1_row[:, :],
                                         ALU.mult, ALU.mult).then_inc(x_normed, 1)

            def low_hT(c):
                dve.wait_ge(hT_hi_done, c + 1)
                cols = slice(P * c, P * c + P)
                dve.tensor_tensor(hT_lo[:, :, cols], turned_two[c % 2], hT_hi[:, :, cols].bitcast(F32),
                                  ALU.subtract).then_inc(hT_lo_done, 1)

            norm_x(0)
            dve.wait_ge(w_raw_in[1], 16)
            dve.tensor_scalar(w_hi[:, 1], w_raw[:, 1], 1.0, 1.0, ALU.mult, ALU.mult).then_inc(strip1_hi_done, 1)
            dve.wait_ge(strip1_hi_done, 1)
            dve.tensor_tensor(w_lo[:, 1], w_raw[:, 1], w_hi[:, 1].bitcast(F32), ALU.subtract)\
                .then_inc(strip1_split, 1)
            norm_x(1)
            for c in range(2, NT):
                low_hT(c - 2)
                norm_x(c)
            low_hT(NT - 2)
            low_hT(NT - 1)

            dve.wait_ge(rope_parts_in, 16 * 3)
            for n, g in enumerate((gq, gk)):
                dve.tensor_tensor(rope_t[:, n, 0, :, :], rope_in[:, 0, :, :],
                                  g[:, :].unsqueeze(1).to_broadcast([P, NT, HD]), ALU.mult)
                g_b = g[:, :].rearrange("p (a b i) -> p a b i", a=2, b=2)
                for b in range(2):
                    dst = rope_t[:, n, 1, :, :].rearrange("p c (a b i) -> p c a b i", a=2, b=2)[:, :, :, b, :]
                    src = rope_in[:, 1, :, :].rearrange("p c (a b i) -> p c a b i", a=2, b=2)[:, :, :, b, :]
                    last = dve.tensor_tensor(dst, src, g_b[:, :, 1 - b, :].unsqueeze(1)
                                             .to_broadcast([P, NT, 2, HD // 4]), ALU.mult)
            settle(last)

            NH = A_HEADS + A_KV
            dve.wait_ge(proj_read_act, 3 * NT)
            for c in range(NT):
                if c:
                    dve.wait_ge(a_sumsq, c)
                settle(dve.tensor_tensor(t1[:, :, :], zA[:, c], zA[:, c], ALU.mult))
                dve.tensor_reduce(ssqA[:, NH * c:NH * c + NH], t1[:, :, :], AX, ALU.add).then_inc(a_sumsq, 1)
            dve.wait_ge(a_sumsq, NT)
            for c in range(NT):
                dve.wait_ge(a_rstd, c + 1)
                settle(dve.tensor_tensor(zA[:, c], zA[:, c], rstdA[:, NH * c:NH * c + NH].unsqueeze(2)
                                         .to_broadcast([P, NH, HD]), ALU.mult))
                for n, h0, h1 in ((0, 0, A_HEADS), (1, A_HEADS, NH)):
                    nh = h1 - h0
                    dve.tensor_tensor(t1[:, h0:h1, :], zA[:, c, h0:h1, :],
                                      rope_t[:, n, 0, c, :].unsqueeze(1).to_broadcast([P, nh, HD]), ALU.mult)
                    z_b = zA[:, c, h0:h1, :].rearrange("p h (a b i) -> p h a b i", a=2, b=2)
                    t_b = t2[:, h0:h1, :].rearrange("p h (a b i) -> p h a b i", a=2, b=2)
                    s_b = rope_t[:, n, 1, c, :].rearrange("p (a b i) -> p a b i", a=2, b=2)
                    for b in range(2):
                        last = dve.tensor_tensor(t_b[:, :, :, b, :], z_b[:, :, :, 1 - b, :],
                                                 s_b[:, :, b, :].unsqueeze(1).to_broadcast([P, nh, 2, HD // 4]),
                                                 ALU.mult)
                settle(last)
                settle(dve.tensor_tensor(t1[:, :, :], t1[:, :, :], t2[:, :, :], ALU.add))
                if c >= 2:
                    dve.wait_ge(a_turned, 3 * (c - 1))
                q_hi, q_lo = q_parts[:, c % 2, :, 0, :], q_parts[:, c % 2, :, 1, :]
                k_p = k_parts[:, c % 2]
                dve.tensor_copy(q_hi, t1[:, 0:A_HEADS, :])
                dve.tensor_copy(k_p[:, :, 2, :], t1[:, A_HEADS:NH, :])
                settle(dve.tensor_copy(k_p[:, :, 0, :], t1[:, A_HEADS:NH, :]))
                dve.tensor_tensor(q_lo, t1[:, 0:A_HEADS, :], q_hi.bitcast(F32), ALU.subtract)
                dve.tensor_tensor(k_p[:, :, 1, :], t1[:, A_HEADS:NH, :], k_p[:, :, 0, :].bitcast(F32),
                                  ALU.subtract).then_inc(a_parts, 1)
                dve.wait_ge(a_parts, c + 1)

            def norm_probs(u, width):
                dve.wait_ge(exp_done, u + 1)
                settle(dve.reciprocal(column(rinv, u), column(rsum, u)))
                p = probs_of(u)[:, 0:width]
                dve.tensor_scalar(p, p, column(rinv, u), None, ALU.mult).then_inc(probs_normed, 1)

            def low_o(i):
                dve.wait_ge(o_hi_done, i + 1)
                dve.tensor_tensor(oT_lo[:, i, :], tp[2][:, :], oT_hi[:, i, :].bitcast(F32), ALU.subtract)\
                    .then_inc(o_lo_done, 1)

            for u in range(NA + 1):
                if u < NA:
                    dve.wait_ge(score_done, u + 1)
                    dve.tensor_reduce(column(nmax, u), pp[u % 4][:, :], AX, ALU.max, negate=True)\
                        .then_inc(nmax_done, 1)
                if u >= 1:
                    norm_probs(u - 1, SEQ)
                if u >= 12 and u % 8 == 4:
                    low_o(u // 8 - 1)
            low_o(OA - 1)

            dve.wait_ge(dist_in, 16)
            for hp in range(2):
                for kind in "qk":
                    for g in range(NG):
                        n = g_at[("col", kind, g, hp)]
                        dve.wait_ge(col_hi_done, n - N_TOK + 1)
                        src = pp[n % 4]
                        for hh in range(2):
                            half = slice(HD * hh, HD * hh + HD)
                            other = slice(HD - HD * hh, 2 * HD - HD * hh)
                            if kind == "q":
                                last = dve.scalar_tensor_tensor(
                                    qB[other, hh, g, :], src[half, :], SCALE / SLOPES[2 * hp + hh],
                                    qB[half, hh, g, :].bitcast(F32), ALU.mult, ALU.subtract)
                            else:
                                hi = kB[half, hh, g, 0, :].bitcast(F32)
                                dve.tensor_tensor(kB[other, hh, g, 0, :], src[half, :], hi, ALU.subtract)
                                last = dve.tensor_tensor(kB[half, hh, g, 1, :], src[half, :], hi, ALU.subtract)
                        last.then_inc(proj_read_dve, 1)
                first, end = NA + 2 * NT * hp, NA + 2 * NT * (hp + 1)
                for u in range(first, end + 1):
                    if u < end:
                        head, c = divmod(u - NA, NT)
                        dve.wait_ge(score_done, u + 1)
                        wait_probs_free(dve, u)
                        dve.tensor_tensor_reduce(probs_of(u)[:, :], scores_two[u % 2], dist[:, c, :],
                                                 -SLOPES[head], HUGE, ALU.add, ALU.min,
                                                 column(nmax, u)).then_inc(nmax_done, 1)
                    if u > first:
                        norm_probs(u - 1, SEQ + 2 * P)
                low_o(OA + hp)

            for j in range(KC):
                dve.wait_ge(proj_read_act, N_TOK + 2 * (j + 1))
                dve.wait_ge(branch_done, 2 * (j + 1))
                if j:
                    dve.wait_ge(m_hi_done, j)
                    dve.wait_ge(m_lo_done, j)
                for b, m in enumerate((m_a, m_b)):
                    dve.tensor_tensor(m[:, :], stage_e[:, b, :], tp[2 * (j % 2) + b][:, :], ALU.mult)\
                        .then_inc(gates_used, 1)
                dve.wait_ge(gates_used, 2 * (j + 1))
                dve.tensor_tensor(m_a[:, :], m_a[:, :], m_b[:, :], ALU.add).then_inc(merged, 1)
                dve.wait_ge(m_hi_done, j + 1)
                dve.tensor_tensor(mT_lo[:, j, :], m_a[:, :], mT_hi[:, j, :].bitcast(F32), ALU.subtract)\
                    .then_inc(m_lo_done, 1)

            def add_residual(p, c):
                n = g_at[("res", p, c)]
                dve.wait_ge(proj_done, n + 1)
                part = x2[:, c, 2 * P * p:2 * P * (p + 1)]
                dve.tensor_tensor(part, part, pp[n % 4][:, 0:2 * P], ALU.add).then_inc(proj_read_dve, 1)

            def norm_x2(c):
                dve.wait_ge(rstd2, c + 1)
                dve.tensor_scalar(xn[:, c, :], x2[:, c, :], rstd[:, c:c + 1], None, ALU.mult)\
                    .then_inc(xn_done, 1)

            def read_h2(c):
                dve.wait_ge(xn_turned, c + 1)
                if c >= 2:
                    dve.wait_ge(logits_done, c - 1)
                dve.tensor_copy(h2T[:, c % 2, HALF:KC, :],
                                tp[2 * (c % 2) + 1][:, :].rearrange("p (k i) -> p k i", i=P))\
                    .then_inc(h2T_dve_done, 1)

            def route_max(c):
                dve.wait_ge(logits_done, c + 1)
                dve.tensor_reduce(smax[:, c:c + 1], bank[c][:, 0:NE], AX, ALU.max, negate=True)\
                    .then_inc(smax_done, 1)

            def route_norm(c):
                dve.wait_ge(sexp_done, c + 1)
                settle(dve.reciprocal(sinv[:, c:c + 1], ssum[:, c:c + 1]))
                dve.tensor_scalar(aff[:, c, :], logit[:, c, :], sinv[:, c:c + 1], None, ALU.mult)\
                    .then_inc(aff_done, 1)

            dve.wait_ge(router_in, 16 * 2)
            dve.wait_ge(gains_in, 16 * 2)
            dve.tensor_tensor(w_rt[:, :, :], w_rt[:, :, :], g2.unsqueeze(2).to_broadcast([P, KC, NE]),
                              ALU.mult).then_inc(w_rt_scaled, 1)
            dve.wait_ge(x_again_in, 16)
            for group in groups[RES0:RES0 + 12]:
                add_residual(*group[1:])
            norm_x2(0)
            add_residual(2, 2)
            norm_x2(1)
            add_residual(3, 2)
            read_h2(0)
            read_h2(1)
            norm_x2(2)
            route_max(0)
            add_residual(2, 3)
            read_h2(2)
            route_norm(0)
            route_max(1)
            add_residual(3, 3)
            route_norm(1)
            dve.memset(zeros[0:NE, :], 0.0)
            norm_x2(3)
            route_max(2)
            route_norm(2)
            read_h2(3)
            route_max(3)
            route_norm(3)

            dve.wait_ge(route_turned, 1)
            settle(dve.tensor_copy(affT[0:NE, :].rearrange("e (i c) -> e c i", c=NT),
                                   bank[0][0:NE, :].rearrange("e (c i) -> e c i", c=NT)))
            row = affT[0:NE, :]
            for r in range(CAP // 8):
                eight = best[0:NE, 8 * r:8 * r + 8]
                settle(dve.max(eight, row))
                nxt = left[0:NE, r % 2, :]
                settle(dve.match_replace(nxt, eight, row, -1.0))
                row = nxt
            settle(dve.tensor_scalar(taken[0:NE, :], row, 0.0, None, ALU.is_lt))
            settle(dve.tensor_tensor_scan(count[0:NE, :], taken[0:NE, :], zeros[0:NE, :], 0.0, ALU.add, ALU.add))
            dve.tensor_tensor(count[0:NE, :], count[0:NE, :], taken[0:NE, :], ALU.mult).then_inc(pos_done, 1)
            dve.wait_ge(route_turned, 2)
            dve.tensor_copy(pos[:, :, :], bank[1][:, 0:NT * NE].rearrange("p (c e) -> p c e", e=NE))\
                .then_inc(added, 1)
            dve.wait_ge(added, 1)

            with dve.Fori(0, NE // 4) as q:
                wide = [P, NT, 2, CAP]
                place = slot_id[:, :].unsqueeze(1).unsqueeze(1).to_broadcast(wide)
                for pr in range(2):
                    own = pos[:, :, bass.ds(4 * q + 2 * pr, 2)].unsqueeze(3).to_broadcast(wide)
                    dve.tensor_tensor(pick[:, :, 2 * pr:2 * pr + 2, :], place, own, ALU.is_equal)\
                        .then_inc(pick_done, 1)
                dve.wait_ge(pick_done, 3 * q + 2)
                wide = [P, NT, 4, CAP]
                dve.tensor_tensor(pick_g[:, :, :, :], pick[:, :, :, :],
                                  aff[:, :, bass.ds(4 * q, 4)].unsqueeze(3).to_broadcast(wide), ALU.mult)\
                    .then_inc(pick_done, 1)
                for pr in range(2):
                    dve.wait_ge(give_turned, 2 * q + (pr + 1))
                    dve.tensor_copy(give[:, pr, :], bank[6 + pr][:, :]).then_inc(give_done, 1)
                for i in range(4):
                    dve.wait_ge(sig_done, 4 * q + (i + 1))
                    if i:
                        dve.wait_ge(act_turned, 4 * q + i)
                    dve.tensor_tensor(act[:, :], sig[:, :], bank[0][:, :], ALU.mult).then_inc(silu_half, 1)
                    dve.wait_ge(silu_half, 4 * q + (i + 1))
                    dve.wait_ge(w_slot_used[slot_of(i, 3)], ROUNDS * q + slot_round(i, 3))
                    dve.tensor_tensor(act[:, :], act[:, :], bank[1][:, :], ALU.mult).then_inc(act_done, 1)
                    if i % 2:
                        for n in range(8):
                            c, f = divmod(n, 2)
                            dve.wait_ge(scattered, 16 * q + (8 * (i // 2) + n + 1))
                            part = x2[:, c, SEQ * f:SEQ * f + SEQ]
                            dve.tensor_tensor(part, part, bank[6 + n % 2][:, :], ALU.add).then_inc(added, 1)

            dve.wait_ge(gf_in, 16)
            for c in range(NT):
                dve.wait_ge(rstd3, c + 1)
                dve.scalar_tensor_tensor(fin[:, c, :], x2[:, c, :], rstd[:, c:c + 1], gf[:, :],
                                         ALU.mult, ALU.mult).then_inc(fin_done, 1)


_INS = ["x", "norm1_g", "w_in", "b_gates", "q_norm_g", "k_norm_g", "w_o_a", "w_o_b", "w_out", "norm2_g",
        "w_router", "w_gate", "w_up", "w_down", "normf_g"]


def shape_constants():
    f = np.float32
    token = NT * np.arange(P)[:, None] + np.arange(NT)[None, :]
    half = HD // 2
    inv_freq = f(1.0) / (f(ROPE_THETA) ** (np.arange(0, half, 2, dtype=f) / f(half)))
    rope = np.zeros((P, 2, NT, 2, 2, HD // 4), f)
    for a, coord in enumerate((token // GRID_W, token % GRID_W)):
        angle = coord.astype(f)[..., None] * inv_freq
        rope[:, 0, :, a, :, :] = np.cos(angle)[:, :, None, :]
        rope[:, 1, :, a, 0, :] = -np.sin(angle)
        rope[:, 1, :, a, 1, :] = np.sin(angle)
    distance = np.zeros((P, NT, SEQ + 2 * P), f)
    i, j = np.arange(P)[:, None], np.arange(P)[None, :]
    for c in range(NT):
        for k in range(NT):
            far = np.abs(NT * (i - j) + c - k)
            distance[:, c, P * k:P * k + P] = -np.where(far <= B_GROUPS[0][0] // 2, far, FAR)
    for g in (1, 2):
        window, dil = B_GROUPS[g]
        far = NT * np.abs(i - j)
        share = SLOPES[g * B_HPG] / SLOPES[0]
        distance[:, :, SEQ + P * (g - 1):SEQ + P * g] = -np.where(
            (far <= window // 2) & (far % dil == 0), far * share, FAR)[:, None, :]
    slots = np.tile(np.arange(1, CAP + 1, dtype=f), (P, 1))
    return {"identity": np.eye(P, dtype=f), "rope": rope.reshape(P, 2, NT, HD), "distance": distance,
            "slots": slots}


def kernel(**inputs):
    import concourse.bacc as _bacc
    from concourse.bass_utils import run_bass_kernel_spmd as _run

    nc = _bacc.Bacc("TRN2", target_bir_lowering=False, num_devices=1)
    given = {name: np.ascontiguousarray(inputs[name]) for name in _INS} | shape_constants()
    arrays, args = {}, {}
    for name, a in given.items():
        arrays[f"in_{name}"] = a
        args[name] = nc.dram_tensor(f"in_{name}", a.shape, mybir.dt.from_np(a.dtype), kind="ExternalInput").ap()
    out = nc.dram_tensor("out", (1, SEQ, D), F32, kind="ExternalOutput").ap()
    encoder_block(nc, out=out, **args)
    r = _run(nc, [arrays], core_ids=[0])
    return r.results[0]["out"]
```

```python
import math
from contextlib import ExitStack

import numpy as np

import concourse.bass as bass
from concourse import mybir

ALU = mybir.AluOpType
ACT = mybir.ActivationFunctionType
F32 = mybir.dt.float32
F32R = mybir.dt.float32r
AX = mybir.AxisListType.X

P = 128
SEQ = 512
D = 1024
NT = SEQ // P
KC = D // P
HD = 64
A_HEADS, A_KV = 8, 2
B_GROUPS = ((128, 1), (512, 4), (2048, 16))
NG = len(B_GROUPS)
B_HPG = 4
B_HEADS = NG * B_HPG
A_Q_W, A_KV_W, B_W = A_HEADS * HD, A_KV * HD, B_HEADS * HD
NE = 16
FF = 1024
CAP = 2 * SEQ // NE
EPS = 1e-6
GRID_W = 64
ROPE_THETA = 10000.0
FAR = 1e32
HUGE = 3e38
KIB = 1024

COL_A = 0
COL_BQ = A_Q_W + 2 * A_KV_W
COL_BK = COL_BQ + B_W
COL_BV = COL_BK + B_W
COL_GA = COL_BV + B_W
COL_GB = COL_GA + D
RING = 4
SLOTS = 8
SCALE = HD ** -0.5
SLOPES = [2.0 ** (-8.0 * (i + 1) / B_HEADS) for i in range(B_HEADS)]


def strips_in_order():
    out = [("a", i) for i in range((A_Q_W + 2 * A_KV_W) // P)]
    out += [("v", i) for i in range(B_W // P)]
    for hp in range(B_HPG // 2):
        out += [(kind, g, hp) for kind in "qk" for g in range(NG)]
    for j in range(KC):
        out += [("ga", j), ("gb", j), ("wo", j)]
    return out + [("out", i) for i in range(D // P)]


def encoder_block(nc, x, norm1_g, w_in, b_gates, q_norm_g, k_norm_g, w_o_a, w_o_b, w_out, norm2_g,
                  w_router, w_gate, w_up, w_down, normf_g, identity, rope, distance, slots, out):
    strips = strips_in_order()
    at = {s: n for n, s in enumerate(strips)}
    w_in_k = w_in[0].rearrange("(k p) n -> p k n", p=P)
    w_oa_k = w_o_a[0].rearrange("(k p) n -> p k n", p=P)
    w_ob_k = w_o_b[0].rearrange("(k p) n -> p k n", p=P)
    w_out_k = w_out[0].rearrange("(k p) n -> p k n", p=P)
    x_t = x[0].rearrange("(i c) d -> i c d", c=NT)
    out_t = out[0].rearrange("(i c) d -> i c d", c=NT)
    OA, OB = A_Q_W // P, B_HPG * HD // P

    base = (nc.sbuf_base + 31) // 32 * 32

    def sb(name, shape, kib, dt=F32):
        return nc.alloc_sbuf_tensor_at(name, [P] + shape, dt, offset=base + int(kib * KIB))

    hT_hi = sb("hT_hi", [KC, SEQ], 0, F32R)
    hT_lo = sb("hT_lo", [KC, SEQ], 16, F32R)
    w_raw = sb("w_raw", [RING, KC, P], 32)
    w_hi = sb("w_hi", [RING, KC, P], 48, F32R)
    w_lo = sb("w_lo", [RING, KC, P], 64, F32R)
    oT_hi = sb("oT_hi", [OA + OB, SEQ], 80, F32R)
    oT_lo = sb("oT_lo", [OA + OB, SEQ], 92, F32R)
    ident = sb("ident", [P], 104)
    small = sb("small", [256], 104.5)
    rope_t = sb("rope_t", [2, 2, NT, HD], 105.5)
    W0 = 111.5
    x_in = sb("x_in", [NT, D], W0)
    g1_row = sb("g1_row", [D], W0 + 24)
    rope_in = sb("rope_in", [2, NT, HD], W0 + 16)
    t1 = sb("t1", [A_HEADS + A_KV, HD], W0 + 16)
    t2 = sb("t2", [A_HEADS + A_KV, HD], W0 + 18.5)
    pT = sb("pT", [2, NT, SEQ], W0)
    probs_a = [sb(f"probs_a{i}", [SEQ], W0 + 16 + 2 * i) for i in range(3)]
    probs_b = [sb(f"probs_b{i}", [SEQ + 2 * P], W0 + at_) for i, at_ in enumerate((16, 19, 56))]
    vB = sb("vB", [NT, B_W], W0 + 22)
    vA = sb("vA", [NT, A_KV_W], W0 + 34)
    qA = sb("qA", [A_HEADS, SEQ], W0 + 36, F32R)
    kA = sb("kA", [A_KV, 2, SEQ], W0 + 52, F32R)
    dist = sb("dist", [NT, SEQ + 2 * P], W0 + 36)
    pT_dil = sb("pT_dil", [2, 2, SEQ], W0 + 48)
    q_parts = sb("q_parts", [2, A_HEADS, 2, HD], W0, F32R)
    k_parts = sb("k_parts", [2, A_KV, 3, HD], W0 + 8, F32R)
    squares = sb("squares", [D], W0 + 60)
    zA = sb("zA", [NT, A_HEADS + A_KV, HD], W0 + 60)
    qB = sb("qB", [NG, 2, SEQ], W0 + 60, F32R)
    kB = sb("kB", [2, NG, 2, SEQ], W0 + 72, F32R)
    qB_next = sb("qB_next", [2, SEQ], 105.5, F32R)
    stage_e = sb("stage_e", [2, SEQ], W0 + 60)
    m_a = sb("m_a", [SEQ], W0 + 48)
    m_b = sb("m_b", [SEQ], W0 + 50)
    mT_hi = sb("mT_hi", [KC, SEQ], W0 + 64, F32R)
    mT_lo = sb("mT_lo", [KC, SEQ], W0 + 80, F32R)
    x2 = sb("x2", [NT, D], 80)
    xn = sb("xn", [NT, D], 32)
    h2T = sb("h2T", [2, KC, P], 96)
    aff = sb("aff", [NT, NE], 109.5)
    pos = sb("pos", [NT, NE], 109.75)
    slot_id = sb("slot_id", [CAP], 110)
    logit = sb("logit", [NT, NE], 110.25)
    w_rt = sb("w_rt", [KC, NE], 110.5)
    affT = sb("affT", [SEQ], 48)
    left = sb("left", [2, SEQ], 50)
    taken = sb("taken", [SEQ], 54)
    count = sb("count", [SEQ], 56)
    zeros = sb("zeros", [SEQ], 58)
    best = sb("best", [CAP], 60)
    HALF = KC // 2
    wslot = [sb(f"wslot{i}", [HALF, D], kib) for i, kib in
             enumerate((W0, W0 + 16, W0 + 32, W0 + 48, 0, 16, W0 + 64, W0 + 80, 64))]
    give = sb("give", [2, SEQ], 48, F32R)
    xinT = sb("xinT", [KC, 2 * CAP], 52)
    y_hi = sb("y_hi", [D], 56, F32R)
    y_lo = sb("y_lo", [D], 60, F32R)
    actT = sb("actT", [2, NT, P], 96)
    pick = sb("pick", [NT, 4, CAP], 100)
    act = sb("act", [2, SEQ], 105.5)
    slot_aff = sb("slot_aff", [2], 111.25)
    gf = sb("gf", [D], 100)
    fin = sb("fin", [NT, D], 32)

    g2 = small[:, 8:16]
    bg = small[:, 16:32]
    ssq, rstd = small[:, 32:36], small[:, 36:40]
    neg_half = small[:, 40:80]
    ssqA, rstdA = small[:, 80:120], small[:, 120:160]
    nmax, rsum, rinv = small[:, 160:164], small[:, 164:168], small[:, 168:172]
    smax, ssum, sinv = small[:, 172:176], small[:, 176:180], small[:, 180:184]
    ssq_half = small[:, 184:192]
    gq, gk = sb("gq", [HD], W0 + 70), sb("gk", [HD], W0 + 70.25)

    with ExitStack() as ctx:
        def sem(name):
            return ctx.enter_context(nc.semaphore(name))

        psum = ctx.enter_context(nc.psum_tensor("psum", [P, 8, 512], F32))
        bank = [psum[:, i, :] for i in range(8)]
        scores_two = [psum[:, 2 * i:2 * i + 2, :].rearrange("p b n -> p (b n)")[:, 0:SEQ + 2 * P]
                      for i in range(2)]
        turned_two = [psum[:, 4 + 2 * i:6 + 2 * i, :].rearrange("p b (k i) -> p (b k) i", i=P)
                      for i in range(2)]
        pp = bank[0:4]
        tp = bank[4:8]

        ident_in = sem("ident_in")
        g1_in = sem("g1_in")
        rope_parts_in = sem("rope_parts_in")
        gains_in = sem("gains_in")
        x_tile_in = [sem(f"x_tile_in{c}") for c in range(NT)]
        x_again_in = sem("x_again_in")
        dist_in = sem("dist_in")
        w_raw_in = [sem(f"w_raw_in{i}") for i in range(RING)]
        w_split = sem("w_split")
        w_hi_done = sem("w_hi_done")
        dve_hi_done = sem("dve_hi_done")
        dve_split = sem("dve_split")
        neg_half_set = sem("neg_half_set")
        sumsq_done = sem("sumsq_done")
        ms_done = sem("ms_done")
        rstd_done = sem("rstd_done")
        x_normed = sem("x_normed")
        x_turned = sem("x_turned")
        hT_hi_done = sem("hT_hi_done")
        hT_lo_done = sem("hT_lo_done")
        proj_done = sem("proj_done")
        proj_read_act = sem("proj_read_act")
        proj_read_dve = sem("proj_read_dve")
        dve_step = sem("dve_step")
        first_gates_open = sem("first_gates_open")
        a_sumsq = sem("a_sumsq")
        a_ms = sem("a_ms")
        a_rstd = sem("a_rstd")
        a_parts = sem("a_parts")
        a_turned = sem("a_turned")
        a_turned_read = sem("a_turned_read")
        score_done = sem("score_done")
        nmax_done = sem("nmax_done")
        exp_done = sem("exp_done")
        probs_normed = sem("probs_normed")
        probs_turned = sem("probs_turned")
        pT_done = sem("pT_done")
        pv_done = sem("pv_done")
        o_hi_done = sem("o_hi_done")
        o_lo_done = sem("o_lo_done")
        col_hi_done = sem("col_hi_done")
        branch_done = sem("branch_done")
        gates_used = sem("gates_used")
        merged = sem("merged")
        silu_half = sem("silu_half")
        m_hi_done = sem("m_hi_done")
        m_lo_done = sem("m_lo_done")
        w_slot_in = [[sem(f"w_slot{i}_{part}_in") for part in ("first", "second")] for i in range(SLOTS + 1)]
        w_slot_used = [sem(f"w_slot_used{i}") for i in range(SLOTS + 1)]
        router_in = sem("router_in")
        gf_in = sem("gf_in")
        sumsq2 = sem("sumsq2")
        rstd2 = sem("rstd2")
        xn_done = sem("xn_done")
        x2_turned = sem("x2_turned")
        h2T_act_done = sem("h2T_act_done")
        h2T_dve_done = sem("h2T_dve_done")
        w_rt_scaled = sem("w_rt_scaled")
        logits_done = sem("logits_done")
        route_turned = sem("route_turned")
        smax_done = sem("smax_done")
        sexp_done = sem("sexp_done")
        aff_done = sem("aff_done")
        eight_taken = sem("eight_taken")
        pos_done = sem("pos_done")
        pick_done = sem("pick_done")
        gathered = sem("gathered")
        xin_done = sem("xin_done")
        give_turned = sem("give_turned")
        give_done = sem("give_done")
        sig_done = sem("sig_done")
        act_done = sem("act_done")
        act_turned = sem("act_turned")
        actT_done = sem("actT_done")
        slot_aff_turned = sem("slot_aff_turned")
        slot_aff_done = sem("slot_aff_done")
        y_hi_done = sem("y_hi_done")
        y_lo_done = sem("y_lo_done")
        scattered = sem("scattered")
        added = sem("added")
        ssq3 = sem("ssq3")
        ssq3_summed = sem("ssq3_summed")
        rstd3 = sem("rstd3")
        fin_done = sem("fin_done")
        out_written = sem("out_written")

        groups = [("tok", kind, p, c) for kind in "av" for p in range(3) for c in range(NT)]
        groups += [("col",) + s for s in strips if s[0] in "qk"]
        groups += [("gate", j, b) for j in range(KC) for b in range(2)]
        groups += [("res", p, c) for p in (0, 1) for c in range(NT)]
        groups += [("res", p, c) for p, c in ((2, 0), (2, 1), (3, 0), (3, 1), (2, 2), (3, 2), (2, 3), (3, 3))]
        g_at = {g: n for n, g in enumerate(groups)}
        bank_of = [n % 4 for n, g in enumerate(groups) if g[0] == "tok"]
        bank_of += [3, 5, 3, 5, 3, 5] + [6, 6, 0, 1, 2, 3] + [6, 6] + [i % 4 for i in range(2 * KC - 2)]
        bank_of += [i % 4 for i in range(D // P // 2 * NT)]
        by_act = [g[0] in ("tok", "gate") for g in groups]

        NA = A_HEADS * NT
        N_RES = D // P // 2 * NT
        RES0 = g_at[("res", 0, 0)]
        N_COL = 2 * NG * 2
        N_TOK = 6 * NT

        def probs_of(u):
            return (probs_a if u < NA else probs_b)[u % 3]

        def wait_probs_free(eng, u):
            before = u - 3 if u < NA else max(u - 3, NA - 1)
            if before >= 0:
                eng.wait_ge(probs_turned, before + 1)

        def column(of, u):
            return of[:, u % 4:u % 4 + 1]

        def tile_summed(eng, c):
            eng.wait_ge(proj_read_dve, N_COL + g_at[("res", 3, c)] - RES0 + 1)

        HALVES = [(w, h, e) for e in range(2) for h in range(2) for w in (w_gate, w_up)]
        HALVES += [(w_down, h, e) for h in range(2) for e in range(2)]
        QUAD = 2 * len(HALVES)

        def half_at(pr, entry):
            return len(HALVES) * pr + HALVES.index(entry)

        def slot_of(first, m):
            return m if first and m <= SLOTS else (m - 1) % SLOTS

        def slot_round(first, q, m):
            return 1 if first and m <= SLOTS else QUAD // SLOTS * q + (m - 1) // SLOTS + 1

        col_groups = [g for g in groups if g[0] == "col"]
        A_FILL = [min(2 * NG * KC, (i + 1) * 2 * NG * KC // (NA - 1)) for i in range(NA)]
        B_FILL = [3, 6, 8, 8, 11, 14, 16, 16]

        def filled_at(plan, g):
            return next(i for i, steps in enumerate(plan) if steps >= KC * (g + 1))

        def q_of(hp, hh, g):
            if hp and g == 0:
                return qB_next[:, hh, :]
            if hp and g == 1:
                return (oT_hi, oT_lo)[hh][:, OA + 1, :]
            return qB[:, g, hh, :]

        BY_DVE = (1, len(strips) - 1)

        def wait_split(eng, n):
            if n in BY_DVE:
                eng.wait_ge(dve_split, BY_DVE.index(n) + 1)
            else:
                eng.wait_ge(w_split, n + 1 - sum(m < n for m in BY_DVE))

        def wait_used(eng, n):
            kind, i = strips[n][0:2]
            if kind in "av":
                eng.wait_ge(proj_done, g_at[("tok", kind, i // 2, NT - 1)] + 1)
            elif kind in "qk":
                eng.wait_ge(proj_done, g_at[("col",) + strips[n]] + 1)
            elif kind == "wo":
                eng.wait_ge(branch_done, 2 * (i + 1))
            elif kind == "out":
                eng.wait_ge(proj_done, g_at[("res", i // 2, NT - 1)] + 1)
            else:
                eng.wait_ge(proj_done, g_at[("gate", i, int(kind == "gb"))] + 1)

        block = ctx.enter_context(nc.Block())

        @block.sync
        def _(sp):
            def load_x(c):
                sp.dma_start(x_in[:, c, :], x_t[:, c, :]).then_inc(x_tile_in[c], 16)

            def load_strip(n):
                s = strips[n]
                if n >= RING:
                    wait_split(sp, n - RING)
                raw = w_raw[:, n % RING]
                done = w_raw_in[n % RING]
                if s[0] == "wo":
                    cols = slice(P * s[1], P * (s[1] + 1))
                    sp.dma_start(raw[:, 0:OA, :], w_oa_k[:, :, cols]).then_inc(done, 16)
                    sp.dma_start(raw[:, OA:OA + OB, :], w_ob_k[:, :, cols]).then_inc(done, 16)
                    return
                if s[0] == "out":
                    sp.dma_start(raw, w_out_k[:, :, P * s[1]:P * (s[1] + 1)]).then_inc(done, 16)
                    return
                if s[0] == "q":
                    col = COL_BQ + (s[1] * B_HPG + 2 * s[2]) * HD
                elif s[0] == "k":
                    col = COL_BK + (s[1] * B_HPG + 2 * s[2]) * HD
                else:
                    col = {"a": COL_A, "v": COL_BV, "ga": COL_GA, "gb": COL_GB}[s[0]] + P * s[1]
                sp.dma_start(raw, w_in_k[:, :, col:col + P]).then_inc(done, 16)

            QUARTER = HALF // 2

            def load_part(slot, m, q, part):
                pr, entry = divmod(m, len(HALVES))
                matrix, h, e = HALVES[entry]
                rows = matrix[0, 4 * q + 2 * pr + e].rearrange("(h k p) n -> h p k n", h=4, p=P)[2 * h + part]
                sp.dma_start(wslot[slot][:, QUARTER * part:QUARTER * (part + 1), :], rows)\
                    .then_inc(w_slot_in[slot][part], 16)

            def load_slot(slot, m, q):
                load_part(slot, m, q, 0)
                load_part(slot, m, q, 1)

            load_x(0)
            for n in range(len(strips)):
                load_strip(n)
                if n == 0:
                    load_x(1)
                if n == 1:
                    for c in range(2, NT):
                        load_x(c)
                if strips[n] in (("wo", 2), ("wo", 3), ("wo", 4)):
                    sp.wait_ge(pv_done, OA + OB)
                    load_slot(strips[n][1] - 2, strips[n][1] - 2, 0)
                if strips[n] == ("out", 3):
                    sp.wait_ge(branch_done, 2 * KC)
                    sp.dma_start(x2[:, :, :], x_t).then_inc(x_again_in, 16)
                    sp.wait_ge(proj_done, g_at[("gate", KC - 1, 1)] + 1)
                    load_slot(4, 4, 0)
                if strips[n] == ("out", 5):
                    load_slot(5, 5, 0)
            sp.wait_ge(m_hi_done, KC)
            sp.wait_ge(m_lo_done, KC)
            load_slot(3, 3, 0)
            sp.wait_ge(proj_done, len(groups))
            for i in (6, 7, 8):
                load_slot(i, i, 0)

            def load_again(q, m):
                if HALVES[m % len(HALVES)][0] is not w_down:
                    wait_free(q, m)
                    load_slot((m - 1) % SLOTS, m, q)
                elif HALVES[m % len(HALVES)][2] == 0:
                    for part in range(2):
                        for m_ in (m, m + 1):
                            if part == 0:
                                wait_free(q, m_)
                            load_part((m_ - 1) % SLOTS, m_, q, part)

            def wait_free(q, m):
                sp.wait_ge(w_slot_used[(m - 1) % SLOTS], QUAD // SLOTS * q + (m - 1) // SLOTS)

            for m in range(SLOTS + 1, len(HALVES)):
                wait_free(0, m)
                load_slot(m - SLOTS - 1, m, 0)
            with sp.Fori(0, NE // 4 - 1) as q:
                for m in range(len(HALVES), QUAD + len(HALVES)):
                    load_again(q, m)
            for m in range(len(HALVES), QUAD):
                load_again(NE // 4 - 1, m)
            for n in range(2 * NT):
                c, f = divmod(n, 2)
                cols = slice(SEQ * f, SEQ * f + SEQ)
                sp.wait_ge(fin_done, n + 1)
                sp.dma_start(out_t[:, c, cols], fin[:, c, cols]).then_inc(out_written, 16)
            sp.wait_ge(out_written, 16 * 2 * NT)

        @block.gpsimd
        def _(pool):
            pool.memset(neg_half, -0.5).then_inc(neg_half_set, 1)
            pool.wait_ge(neg_half_set, 1)

            def power(sums, into, n, width, counted, done, first):
                pool.tensor_scalar(into, sums, 1.0 / width, EPS, ALU.mult, ALU.add).then_inc(counted, 1)
                pool.wait_ge(counted, first + 1)
                pool.tensor_tensor(into, into, neg_half[:, 0:n], ALU.pow).then_inc(done, 1)

            def rstd_of_x(c):
                pool.wait_ge(sumsq_done, c + 1)
                power(ssq[:, c:c + 1], rstd[:, c:c + 1], 1, D, ms_done, rstd_done, c)

            def split_hi(n):
                arrived = sum(2 if t[0] == "wo" else 1 for t in strips[n % RING:n + 1:RING])
                pool.wait_ge(w_raw_in[n % RING], 16 * arrived)
                if n >= RING:
                    wait_used(pool, n - RING)
                k = OA + OB if strips[n][0] == "wo" else KC
                raw, hi = (w[:, n % RING, 0:k, :] for w in (w_raw, w_hi))
                pool.tensor_scalar(hi, raw, 1.0, 1.0, ALU.mult, ALU.mult).then_inc(w_hi_done, 1)

            def split_lo(n):
                pool.wait_ge(w_hi_done, n + 1 - sum(m < n for m in BY_DVE))
                k = OA + OB if strips[n][0] == "wo" else KC
                raw, hi, lo = (w[:, n % RING, 0:k, :] for w in (w_raw, w_hi, w_lo))
                pool.tensor_tensor(lo, raw, hi.bitcast(F32), ALU.subtract).then_inc(w_split, 1)

            rstd_of_x(0)
            split_hi(0)
            split_lo(0)
            for c in range(1, NT):
                rstd_of_x(c)
            for n in range(2, len(strips) - 1):
                if n == at[("v", 4)]:
                    w = A_HEADS + A_KV
                    for c in range(NT):
                        pool.wait_ge(a_sumsq, c + 1)
                        power(ssqA[:, w * c:w * c + w], rstdA[:, w * c:w * c + w], w, HD, a_ms, a_rstd, c)
                split_hi(n)
                split_lo(n)

            for c in range(NT):
                pool.wait_ge(sumsq2, c + 1)
                power(ssq[:, c:c + 1], rstd[:, c:c + 1], 1, D, ms_done, rstd2, NT + c)
            for c in range(NT):
                pool.wait_ge(ssq3, NT + c + 1)
                pool.tensor_tensor(ssq[:, c:c + 1], ssq_half[:, c:c + 1], ssq_half[:, NT + c:NT + c + 1],
                                   ALU.add).then_inc(ssq3_summed, 1)
                pool.wait_ge(ssq3_summed, c + 1)
                power(ssq[:, c:c + 1], rstd[:, c:c + 1], 1, D, ms_done, rstd3, 2 * NT + c)

        @block.scalar
        def _(act_):
            act_.dma_start(ident[:, :], identity).then_inc(ident_in, 16)
            act_.dma_start(g1_row[:, :], norm1_g[0].partition_broadcast(P)).then_inc(g1_in, 16)

            def square_x(c):
                act_.wait_ge(x_tile_in[c], 16)
                if c:
                    act_.wait_ge(sumsq_done, c)
                act_.activation(squares[:, :], x_in[:, c, :], ACT.Square,
                                accum_out=ssq[:, c:c + 1]).then_inc(sumsq_done, 1)

            def high_hT(c):
                act_.wait_ge(x_turned, c + 1)
                act_.activation(hT_hi[:, :, P * c:P * c + P], turned_two[c % 2], ACT.Copy).then_inc(hT_hi_done, 1)

            square_x(0)
            act_.dma_start(rope_in[:, :, :, :], rope).then_inc(rope_parts_in, 16)
            for dst, src in ((gq, q_norm_g), (gk, k_norm_g)):
                act_.dma_start(dst[:, :], src[0].partition_broadcast(P)).then_inc(rope_parts_in, 16)
            for c in range(1, NT):
                square_x(c)
                high_hT(c - 1)
            high_hT(NT - 1)
            for dst, src in ((g2, norm2_g[0]), (bg, b_gates[0])):
                act_.dma_start(dst, src.rearrange("(k p) -> p k", p=P),
                               allow_slow_non_contiguous=True).then_inc(gains_in, 16)
            act_.dma_start(w_rt[:, :, :], w_router[0].rearrange("(k p) e -> p k e", p=P)).then_inc(router_in, 16)
            act_.dma_start(slot_id[:, :], slots).then_inc(router_in, 16)

            def read_tok(kind, p, c):
                n = g_at[("tok", kind, p, c)]
                src = bank[bank_of[n]][:, 0:2 * P]
                act_.wait_ge(proj_done, n + 1)
                if kind == "v":
                    act_.activation(vB[:, c, 2 * P * p:2 * P * (p + 1)], src, ACT.Copy)\
                        .then_inc(proj_read_act, 1)
                elif p < 2:
                    act_.activation(zA[:, c, 4 * p:4 * p + 4, :], src.rearrange("p (h d) -> p h d", d=HD),
                                    ACT.Copy).then_inc(proj_read_act, 1)
                else:
                    act_.activation(zA[:, c, 8:10, :], src[:, 0:P].rearrange("p (h d) -> p h d", d=HD), ACT.Copy)
                    act_.activation(vA[:, c, :], src[:, P:2 * P], ACT.Copy).then_inc(proj_read_act, 1)

            def read_turned(c):
                for b in range(3):
                    n = 3 * c + b
                    act_.wait_ge(a_turned, n + 1)
                    src = tp[n % 4][:, :].rearrange("p (h i) -> p h i", i=P)
                    cols = slice(P * c, P * c + P)
                    if b < 2:
                        act_.activation(qA[:, 4 * b:4 * b + 4, cols], src, ACT.Copy, scale=SCALE)\
                            .then_inc(a_turned_read, 1)
                    else:
                        dst = kA[:, :, :, cols].rearrange("p k v i -> p (k v) i")
                        act_.activation(dst, src, ACT.Copy).then_inc(a_turned_read, 1)

            for kind, p in (("a", 0), ("a", 1), ("a", 2), ("v", 0), ("v", 1)):
                for c in range(NT):
                    read_tok(kind, p, c)
            read_turned(0)
            read_tok("v", 2, 0)
            read_tok("v", 2, 1)
            read_turned(1)
            read_tok("v", 2, 2)
            read_tok("v", 2, 3)
            read_turned(2)
            read_turned(3)

            def soft_exp(u, width, src):
                act_.wait_ge(nmax_done, u + 1)
                wait_probs_free(act_, u)
                act_.activation(probs_of(u)[:, 0:width], src, ACT.Exp, bias=column(nmax, u),
                                scale=1.0 if u < NA else -1.0,
                                accum_out=column(rsum, u)).then_inc(exp_done, 1)

            def read_probs(u):
                head, c = divmod(u, NT)
                cols = slice(P * c, P * c + P)
                if head >= 2:
                    act_.wait_ge(pv_done, head // 2)
                act_.wait_ge(probs_turned, u + 1)
                last = act_.activation(pT[:, head % 2, :, cols],
                                       tp[(0, 3)[u % 2]][:, :].rearrange("p (k i) -> p k i", i=P), ACT.Copy)
                if u >= NA:
                    last = act_.activation(pT_dil[:, head % 2, :, cols],
                                           tp[1][:, 0:2 * P].rearrange("p (g i) -> p g i", i=P), ACT.Copy)
                last.then_inc(pT_done, 1)

            def read_o(i):
                act_.wait_ge(pv_done, i + 1)
                act_.activation(oT_hi[:, i, :], tp[2][:, :], ACT.Copy).then_inc(o_hi_done, 1)

            def high_col(g, hh):
                _, kind, grp, hp = col_groups[g]
                act_.wait_ge(proj_done, N_TOK + g + 1)
                src = bank[bank_of[N_TOK + g]]
                half = slice(HD * hh, HD * hh + HD)
                other = slice(HD - HD * hh, 2 * HD - HD * hh)
                if kind == "q":
                    last = act_.activation(q_of(hp, hh, grp)[half, :], src[half, :], ACT.Copy,
                                           scale=SCALE / SLOPES[2 * hp + hh])
                else:
                    act_.activation(kB[half, hh, grp, 0, :], src[half, :], ACT.Copy)
                    last = act_.activation(kB[other, hh, grp, 1, :], src[half, :], ACT.Copy)
                last.then_inc(col_hi_done, 1)

            for u in range(NA + 4):
                if u < NA:
                    soft_exp(u, SEQ, pp[u % 3][:, :])
                    if u == NA - 1:
                        act_.dma_start(dist[:, :, :], distance).then_inc(dist_in, 16)
                if 2 <= u < NA + 2:
                    read_probs(u - 2)
                for g in range(2 * NG):
                    for hh in range(2):
                        if u == filled_at(A_FILL, g) + 2 + hh:
                            high_col(g, hh)
                if u >= 10 and u % 8 == 2 and u < NA:
                    read_o(u // 8 - 1)
            read_o(OA - 1)

            for hp in range(2):
                first, end = NA + 2 * NT * hp, NA + 2 * NT * (hp + 1)
                if hp:
                    for g in range(2 * NG + 2, 4 * NG):
                        high_col(g, 0)
                        high_col(g, 1)
                    read_o(OA)
                for u in range(first, end + 2):
                    if u < end:
                        soft_exp(u, SEQ + 2 * P, probs_of(u)[:, :])
                    if u >= first + 2:
                        read_probs(u - 2)
                    for g in range(2):
                        if u == first + filled_at(B_FILL, g) + 2:
                            if hp == 0:
                                high_col(2 * NG + g, 0)
                                high_col(2 * NG + g, 1)
                            else:
                                n = g_at[("gate", 0, g)]
                                act_.wait_ge(proj_done, n + 1)
                                act_.activation(stage_e[:, g, :], bank[bank_of[n]], ACT.Copy)\
                                    .then_inc(proj_read_act, 1)

            act_.wait_ge(gains_in, 16 * 2)
            for b in range(2):
                act_.wait_ge(proj_read_act, N_TOK + b + 1)
                act_.activation(stage_e[:, b, :], stage_e[:, b, :], ACT.Sigmoid,
                                bias=bg[:, KC * b:KC * b + 1]).then_inc(first_gates_open, 1)
            read_o(OA + 1)
            for j in range(KC):
                for b in range(2) if j else ():
                    n = g_at[("gate", j, b)]
                    act_.wait_ge(proj_done, n + 1)
                    act_.wait_ge(gates_used, 2 * j)
                    act_.activation(stage_e[:, b, :], bank[bank_of[n]], ACT.Sigmoid,
                                    bias=bg[:, KC * b + j:KC * b + j + 1]).then_inc(proj_read_act, 1)
                act_.wait_ge(merged, j + 1)
                act_.activation(mT_hi[:, j, :], m_a[:, :], ACT.Copy).then_inc(m_hi_done, 1)

            def square_x2(c):
                tile_summed(act_, c)
                act_.activation(xn[:, c, :], x2[:, c, :], ACT.Square,
                                accum_out=ssq[:, c:c + 1]).then_inc(sumsq2, 1)

            def read_h2(c):
                act_.wait_ge(x2_turned, c + 1)
                if c >= 2:
                    act_.wait_ge(logits_done, c - 1)
                act_.activation(h2T[:, c % 2, 0:HALF, :],
                                tp[2 * (c % 2)][:, :].rearrange("p (k i) -> p k i", i=P), ACT.Copy)\
                    .then_inc(h2T_act_done, 1)

            def route_exp(c):
                act_.wait_ge(smax_done, c + 1)
                act_.activation(logit[:, c, :], logit[:, c, :], ACT.Exp,
                                accum_out=ssum[:, c:c + 1]).then_inc(sexp_done, 1)

            for step, c in ((square_x2, 0), (square_x2, 1), (read_h2, 0), (square_x2, 2), (read_h2, 1),
                            (route_exp, 0), (read_h2, 2), (route_exp, 1), (read_h2, 3), (square_x2, 3),
                            (route_exp, 2), (route_exp, 3)):
                step(c)
            def experts(q, first):
                def read_gathered(pr):
                    for b in range(2):
                        act_.wait_ge(gathered, 4 * q + (2 * pr + b + 1))
                        for k in range(HALF):
                            last = act_.activation(xinT[:, HALF * b + k, :], bank[6 + b][:, P * k:P * k + P],
                                                   ACT.Copy, scale=g2[:, HALF * b + k:HALF * b + k + 1])
                        last.then_inc(xin_done, 1)

                def sigmoid(i):
                    m = half_at(i // 2, (w_gate, 1, i % 2))
                    act_.wait_ge(w_slot_used[slot_of(first, m)], slot_round(first, q, m))
                    if i >= 2 or not first:
                        act_.wait_ge(act_turned, 4 * q + (i - 1))
                    act_.activation(act[:, i % 2, :], bank[4 * (i % 2)][:, :], ACT.Sigmoid).then_inc(sig_done, 1)

                def read_act(i):
                    act_.wait_ge(act_turned, 4 * q + (i + 1))
                    act_.activation(actT[:, i % 2, :, :], bank[2][:, :].rearrange("p (k i) -> p k i", i=P),
                                    ACT.Copy).then_inc(actT_done, 1)

                def high_y(pr):
                    m = half_at(pr, (w_down, 1, 1))
                    act_.wait_ge(w_slot_used[slot_of(first, m)], slot_round(first, q, m))
                    act_.wait_ge(slot_aff_done, 2 * q + 2)
                    act_.wait_ge(added, 16 * q + (8 * pr + 1))
                    for f in range(2):
                        act_.activation(y_hi[:, SEQ * f:SEQ * f + SEQ], bank[(3, 5)[f]][:, :], ACT.Copy,
                                        scale=slot_aff[:, pr:pr + 1]).then_inc(y_hi_done, 1)

                read_gathered(0)
                sigmoid(0)
                sigmoid(1)
                read_act(0)
                read_act(1)
                high_y(0)
                read_gathered(1)
                sigmoid(2)
                sigmoid(3)
                read_act(2)
                read_act(3)
                high_y(1)

            experts(0, True)
            with act_.Fori(1, NE // 4) as q:
                experts(q, False)

            act_.wait_ge(give_turned, NE // 2)
            act_.dma_start(gf[:, :], normf_g.partition_broadcast(P)).then_inc(gf_in, 16)
            for n in range(8):
                f, c = divmod(n, NT)
                cols = slice(SEQ * f, SEQ * f + SEQ)
                act_.wait_ge(added, NE // 2 * 8 - 8 + n + 2)
                act_.activation(fin[:, c, cols], x2[:, c, cols], ACT.Square,
                                accum_out=ssq_half[:, n:n + 1]).then_inc(ssq3, 1)

        @block.tensor
        def _(pe):
            def split_product(out_, k, n_k, stat, mov):
                (s_hi, s_lo), (m_hi, m_lo) = stat, mov
                pe.matmul(out_, s_hi, m_hi, start=(k == 0), stop=False)
                pe.matmul(out_, s_hi, m_lo, start=False, stop=False)
                return pe.matmul(out_, s_lo, m_hi, start=False, stop=(k == n_k - 1))

            def keep_clock(n):
                for _ in range(n):
                    pe.transpose(bank[3][:, 0:P], ident[:, :], ident[:, :])

            def turn_x(c):
                pe.wait_ge(x_normed, c + 1)
                if c >= 2:
                    pe.wait_ge(hT_lo_done, c - 1)
                for k in range(KC):
                    t = pe.transpose(turned_two[c % 2][:, k, :], x_in[:, c, P * k:P * k + P], ident[:, :])
                t.then_inc(x_turned, 1)

            def pp_take(n):
                before = [m for m in range(n) if bank_of[m] == bank_of[n]]
                if before:
                    m = before[-1]
                    if by_act[m]:
                        pe.wait_ge(proj_read_act, sum(by_act[:m + 1]))
                    else:
                        pe.wait_ge(proj_read_dve, m + 1 - sum(by_act[:m + 1]))

            def tok_group(group, n0, act_parts, parts_done=None):
                n, c = g_at[group], group[-1]
                wait_split(pe, n0)
                wait_split(pe, n0 + 1)
                pp_take(n)
                s = n0 % RING
                cols = slice(P * c, P * c + P)
                for k in range(KC):
                    if parts_done is not None:
                        pe.wait_ge(parts_done, k + 1)
                    mm = split_product(bank[bank_of[n]][:, 0:2 * P], k, KC, [t[:, k, cols] for t in act_parts],
                                       [w[:, s:s + 2, k, :] for w in (w_hi, w_lo)])
                mm.then_inc(proj_done, 1)

            def col_steps(group, n0, k0, k1):
                n = g_at[group]
                if k0 == 0:
                    wait_split(pe, n0)
                    pp_take(n)
                for k in range(k0, k1):
                    mm = split_product(bank[bank_of[n]], k, KC, [w[:, n0 % RING, k, :] for w in (w_hi, w_lo)],
                                       [t[:, k, :] for t in (hT_hi, hT_lo)])
                if k1 == KC:
                    mm.then_inc(proj_done, 1)

            def col_group(group, n0):
                col_steps(group, n0, 0, KC)

            def fill(plan, i, todo):
                for step in range(plan[i - 1] if i else 0, plan[i]):
                    col_steps(*todo[step // KC], step % KC, step % KC + 1)

            def turn_a(c):
                pe.wait_ge(a_parts, c + 1)
                for b in range(3):
                    n = 3 * c + b
                    if n >= 4:
                        pe.wait_ge(a_turned_read, n - 3)
                    for i in range(4):
                        src = q_parts[:, c % 2, 4 * b + i, :, :] if b < 2 else \
                            k_parts[:, c % 2, i // 2, i % 2:i % 2 + 2, :]
                        t = pe.transpose(tp[n % 4][:, P * i:P * i + P],
                                         src.rearrange("p a d -> p (a d)").bitcast(F32), ident[:, :])
                    t.then_inc(a_turned, 1)

            hT = (hT_hi, hT_lo)
            pe.wait_ge(ident_in, 16)
            keep_clock(20)
            turn_x(0)
            for c in range(NT):
                if c + 1 < NT:
                    turn_x(c + 1)
                pe.wait_ge(hT_lo_done, c + 1)
                tok_group(("tok", "a", 0, c), at[("a", 0)], hT)
            for kind, p in (("a", 1), ("a", 2), ("v", 0), ("v", 1)):
                for c in range(NT):
                    tok_group(("tok", kind, p, c), at[(kind, 2 * p)], hT)
            turn_a(0)
            tok_group(("tok", "v", 2, 0), at[("v", 4)], hT)
            tok_group(("tok", "v", 2, 1), at[("v", 4)], hT)
            turn_a(1)
            tok_group(("tok", "v", 2, 2), at[("v", 4)], hT)
            tok_group(("tok", "v", 2, 3), at[("v", 4)], hT)
            turn_a(2)
            turn_a(3)

            def scores_a(u):
                h, c = divmod(u, NT)
                if u >= 3:
                    pe.wait_ge(exp_done, u - 2)
                for v in range(2):
                    mm = pe.matmul(pp[u % 3][:, :], qA[:, h, P * c:P * c + P],
                                   kA[:, h // (A_HEADS // A_KV), v, :], start=(v == 0), stop=(v == 1))
                mm.then_inc(score_done, 1)

            def scores_b(u):
                head, c = divmod(u - NA, NT)
                cols = slice(P * c, P * c + P)
                if u >= NA + 2:
                    pe.wait_ge(nmax_done, u - 1)
                for g in range(NG):
                    dst = scores_two[u % 2][:, 0:SEQ] if g == 0 else \
                        scores_two[u % 2][:, SEQ + P * (g - 1):SEQ + P * g]
                    for v in range(2):
                        keys = kB[:, head % 2, g, v, :] if g == 0 else kB[:, head % 2, g, v, cols]
                        mm = pe.matmul(dst, q_of(head // 2, head % 2, g)[:, cols], keys, start=(v == 0), stop=(v == 1))
                mm.then_inc(score_done, 1)

            def turn_probs(u):
                pe.wait_ge(probs_normed, u + 1)
                if u >= NA:
                    pe.wait_ge(pT_done, u)
                    for g in range(2):
                        pe.transpose(tp[1][:, P * g:P * g + P],
                                     probs_of(u)[:, SEQ + P * g:SEQ + P * g + P], ident[:, :])
                elif u >= 2:
                    pe.wait_ge(pT_done, u - 1)
                for k in range(NT):
                    t = pe.transpose(tp[(0, 3)[u % 2]][:, P * k:P * k + P],
                                     probs_of(u)[:, P * k:P * k + P], ident[:, :])
                t.then_inc(probs_turned, 1)

            def values_a(i):
                pe.wait_ge(pT_done, 2 * NT * (i + 1))
                if i:
                    pe.wait_ge(o_lo_done, i)
                kv = 2 * i // (A_HEADS // A_KV)
                for k in range(NT):
                    for hh in range(2):
                        mm = pe.matmul(tp[2][HD * hh:HD * hh + HD, :], vA[:, k, HD * kv:HD * kv + HD],
                                       pT[:, hh, k, :], start=(k == 0), stop=(k == NT - 1))
                mm.then_inc(pv_done, 1)

            def values_b(hp):
                pe.wait_ge(pT_done, NA + 2 * NT * (hp + 1))
                pe.wait_ge(o_lo_done, OA + hp)
                for k in range(NT):
                    for hh in range(2):
                        v0 = HD * (2 * hp + hh)
                        pe.matmul(tp[2][HD * hh:HD * hh + HD, :], vB[:, k, v0:v0 + HD], pT[:, hh, k, :],
                                  start=(k == 0), stop=False, skip_group_check=True)
                for g in range(1, NG):
                    for c in range(NT):
                        for hh in range(2):
                            v0 = HD * (g * B_HPG + 2 * hp + hh)
                            cols = slice(P * c, P * c + P)
                            mm = pe.matmul(tp[2][HD * hh:HD * hh + HD, cols], vB[:, c, v0:v0 + HD],
                                           pT_dil[:, hh, g - 1, cols], start=False, stop=(g == NG - 1),
                                           skip_group_check=True)
                mm.then_inc(pv_done, 1)

            pe.wait_ge(a_turned_read, 3 * NT)
            cols_a = [(g, at[g[1:]]) for g in col_groups[:2 * NG]]
            scores_a(0)
            scores_a(1)
            for u in range(NA):
                if u + 2 < NA:
                    scores_a(u + 2)
                if u > 1 and u % (2 * NT) == 1:
                    values_a(u // (2 * NT) - 1)
                fill(A_FILL, u, cols_a)
                turn_probs(u)
            values_a(OA - 1)
            pe.wait_ge(exp_done, NA)
            pe.wait_ge(proj_read_dve, 2 * NG)
            pe.wait_ge(o_lo_done, OA)
            for hp in range(2):
                todo = [(g, at[g[1:]]) for g in col_groups[2 * NG:2 * NG + 2]] if hp == 0 else \
                    [(("gate", 0, 0), at[("ga", 0)]), (("gate", 0, 1), at[("gb", 0)])]
                first, end = NA + 2 * NT * hp, NA + 2 * NT * (hp + 1)
                scores_b(first)
                scores_b(first + 1)
                for u in range(first, end):
                    if u + 2 < end:
                        scores_b(u + 2)
                    fill(B_FILL, u - first, todo)
                    if u == end - 1:
                        pe.wait_ge(nmax_done, end - 1)
                        if hp == 0:
                            col_group(col_groups[2 * NG + 2], at[col_groups[2 * NG + 2][1:]])
                        else:
                            col_group(("gate", 1, 0), at[("ga", 1)])
                    turn_probs(u)
                pe.wait_ge(nmax_done, end)
                if hp == 0:
                    for g in col_groups[3 * NG:]:
                        col_group(g, at[g[1:]])
                    pe.wait_ge(proj_read_dve, 2 * NG + 2)
                    values_b(0)
                    pe.wait_ge(proj_read_dve, 4 * NG)
                else:
                    pe.wait_ge(proj_read_act, N_TOK + 2)
                    values_b(1)

            for j in range(KC):
                if j:
                    if j > 1:
                        col_group(("gate", j, 0), at[("ga", j)])
                    col_group(("gate", j, 1), at[("gb", j)])
                n0 = at[("wo", j)]
                wait_split(pe, n0)
                if j == 0:
                    pe.wait_ge(o_lo_done, OA + OB)
                if j >= 2:
                    pe.wait_ge(gates_used, 2 * (j - 1))
                for b, (k0, k1) in enumerate(((0, OA), (OA, OA + OB))):
                    for k in range(k0, k1):
                        mm = split_product(tp[2 * (j % 2) + b][:, :], k - k0, k1 - k0,
                                           [w[:, n0 % RING, k, :] for w in (w_hi, w_lo)],
                                           [t[:, k, :] for t in (oT_hi, oT_lo)])
                    mm.then_inc(branch_done, 1)

            def turn_x2(c):
                tile_summed(pe, c)
                if c >= 2:
                    pe.wait_ge(h2T_act_done, c - 1)
                    pe.wait_ge(h2T_dve_done, c - 1)
                for k in range(KC):
                    t = pe.transpose(tp[2 * (c % 2) + k // HALF][:, P * (k % HALF):P * (k % HALF) + P],
                                     x2[:, c, P * k:P * k + P], ident[:, :])
                t.then_inc(x2_turned, 1)

            def route(c):
                pe.wait_ge(h2T_act_done, c + 1)
                pe.wait_ge(h2T_dve_done, c + 1)
                pe.wait_ge(proj_read_dve, N_COL + N_RES - NT + c + 1)
                for k in range(KC):
                    mm = pe.matmul(bank[c][:, 0:NE], h2T[:, c % 2, k, :], w_rt[:, k, :],
                                   start=(k == 0), stop=(k == KC - 1))
                mm.then_inc(logits_done, 1)

            def project(p, c):
                tok_group(("res", p, c), at[("out", 2 * p)], (mT_hi, mT_lo))

            tok_group(groups[RES0], at[("out", 0)], (mT_hi, mT_lo), m_lo_done)
            for group in groups[RES0 + 1:RES0 + 13]:
                project(*group[1:])
            pe.wait_ge(w_rt_scaled, 1)
            turn_x2(0)
            project(3, 2)
            turn_x2(1)
            route(0)
            project(2, 3)
            turn_x2(2)
            route(1)
            project(3, 3)
            turn_x2(3)
            route(2)
            route(3)
            pe.wait_ge(aff_done, NT)
            for c in range(NT):
                t = pe.transpose(bank[0][0:NE, P * c:P * c + P], aff[:, c, :], ident[:, :])
            t.then_inc(route_turned, 1)
            for n in range(CAP // 8):
                pe.wait_ge(eight_taken, n + 1)
                keep_clock(9)
            pe.wait_ge(pos_done, 1)
            for c in range(NT):
                t = pe.transpose(bank[1][:, NE * c:NE * c + NE],
                                 count[0:NE, :].rearrange("e (i c) -> e c i", c=NT)[:, c, :], ident[0:NE, 0:NE])
            t.then_inc(route_turned, 1)

            def experts(q, first):
                def gather(pr, b):
                    pe.wait_ge(pick_done, 2 * q + (pr + 1))
                    if pr:
                        pe.wait_ge(give_done, 2 * q + (b + 1))
                    else:
                        pe.wait_ge(added, 16 * q + 1)
                    for k in range(HALF):
                        for c in range(NT):
                            mm = pe.matmul(bank[6 + b][:, P * k:P * k + P],
                                           xn[:, c, P * (HALF * b + k):P * (HALF * b + k) + P],
                                           pick[:, c, 2 * pr:2 * pr + 2, :],
                                           start=(c == 0), stop=(c == NT - 1))
                    mm.then_inc(gathered, 1)

                def wait_part(m, k):
                    if k % (HALF // 2) == 0:
                        pe.wait_ge(w_slot_in[slot_of(first, m)][k // (HALF // 2)],
                                   16 * slot_round(first, q, m))

                def gate_up(i, h):
                    if h == 0 and (i >= 2 or not first):
                        pe.wait_ge(act_done, 4 * q + (i - 1))
                        if i % 2:
                            pe.wait_ge(y_lo_done, 4 * q + (i - 1))
                    if i % 2 == 0:
                        pe.wait_ge(xin_done, 4 * q + (i + h + 1))
                    for n, w in enumerate((w_gate, w_up)):
                        m = half_at(i // 2, (w, h, i % 2))
                        slot = slot_of(first, m)
                        for k in range(HALF):
                            wait_part(m, k)
                            for f in range(2):
                                mm = pe.matmul(bank[4 * (i % 2) + n][CAP * f:CAP * f + CAP, :],
                                               xinT[:, HALF * h + k, CAP * (i % 2):CAP * (i % 2) + CAP],
                                               wslot[slot][:, k, SEQ * f:SEQ * f + SEQ],
                                               start=(h == 0 and k == 0), stop=(h == 1 and k == HALF - 1))
                        mm.then_inc(w_slot_used[slot], 1)

                def turn_act(i):
                    pe.wait_ge(act_done, 4 * q + (i + 1))
                    if i == 0:
                        pe.wait_ge(slot_aff_done, 2 * q + 2)
                    else:
                        pe.wait_ge(actT_done, 4 * q + i)
                    for k in range(NT):
                        t = pe.transpose(bank[2][:, P * k:P * k + P], act[:, i % 2, P * k:P * k + P], ident[:, :])
                    t.then_inc(act_turned, 1)

                def down(pr):
                    pe.wait_ge(actT_done, 4 * q + (2 * pr + 2))
                    if pr or not first:
                        pe.wait_ge(y_lo_done, 4 * q + 2 * pr)
                    for h in range(2):
                        halves = [half_at(pr, (w_down, h, e)) for e in range(2)]
                        slot = [slot_of(first, m) for m in halves]
                        for k in range(HALF):
                            for m in halves:
                                wait_part(m, k)
                            for f in range(2):
                                for e in range(2):
                                    mm = pe.matmul(bank[(3, 5)[f]][CAP * e:CAP * e + CAP, :],
                                                   actT[:, e, k, CAP * h:CAP * h + CAP],
                                                   wslot[slot[e]][:, k, SEQ * f:SEQ * f + SEQ],
                                                   start=(h == 0 and k == 0), stop=(h == 1 and k == HALF - 1))
                                    if k == HALF - 1 and f == 1:
                                        mm.then_inc(w_slot_used[slot[e]], 1)

                def scatter(pr):
                    pe.wait_ge(give_done, 2 * q + 2)
                    for n in range(8):
                        f, c = divmod(n, NT)
                        if c == 0:
                            pe.wait_ge(y_lo_done, 4 * q + (2 * pr + f + 1))
                        pe.wait_ge(added, 16 * q + (8 * pr + max(n - 1, 0) + 1))
                        for part in (y_hi, y_lo):
                            mm = pe.matmul(bank[6 + n % 2][:, :], give[:, pr, P * c:P * c + P],
                                           part[:, SEQ * f:SEQ * f + SEQ], start=(part is y_hi),
                                           stop=(part is y_lo))
                        mm.then_inc(scattered, 1)

                gather(0, 0)
                pe.wait_ge(pick_done, 2 * q + 2)
                if not first:
                    pe.wait_ge(actT_done, 4 * q)
                for pr in range(2):
                    for c in range(NT):
                        mm = pe.matmul(bank[2][:, 2 * pr:2 * pr + 2], pick[:, c, 2 * pr:2 * pr + 2, :],
                                       aff[:, c, bass.ds(4 * q + 2 * pr, 2)], start=(c == 0), stop=(c == NT - 1))
                mm.then_inc(slot_aff_turned, 1)
                gate_up(0, 0)
                gather(0, 1)
                gate_up(0, 1)
                gate_up(1, 0)
                gate_up(1, 1)
                turn_act(0)
                pe.wait_ge(xin_done, 4 * q + 2)
                for pr in range(2):
                    for c in range(NT):
                        t = pe.transpose(bank[6 + pr][:, P * c:P * c + P],
                                         pick[:, c, 2 * pr:2 * pr + 2, :].rearrange("p a s -> p (a s)"),
                                         ident[:, :])
                    t.then_inc(give_turned, 1)
                turn_act(1)
                down(0)
                gather(1, 0)
                gather(1, 1)
                gate_up(2, 0)
                gate_up(2, 1)
                gate_up(3, 0)
                gate_up(3, 1)
                turn_act(2)
                scatter(0)
                turn_act(3)
                down(1)
                scatter(1)

            experts(0, True)
            with pe.Fori(1, NE // 4) as q:
                experts(q, False)

        @block.vector
        def _(dve):
            steps = [0]

            def settle(ins):
                ins.then_inc(dve_step, 1)
                steps[0] += 1
                dve.wait_ge(dve_step, steps[0])

            dve.wait_ge(g1_in, 16)

            def norm_x(c):
                dve.wait_ge(rstd_done, c + 1)
                dve.scalar_tensor_tensor(x_in[:, c, :], x_in[:, c, :], rstd[:, c:c + 1], g1_row[:, :],
                                         ALU.mult, ALU.mult).then_inc(x_normed, 1)

            def low_hT(c):
                dve.wait_ge(hT_hi_done, c + 1)
                cols = slice(P * c, P * c + P)
                dve.tensor_tensor(hT_lo[:, :, cols], turned_two[c % 2], hT_hi[:, :, cols].bitcast(F32),
                                  ALU.subtract).then_inc(hT_lo_done, 1)

            def split_strip(n):
                if n >= RING:
                    wait_used(dve, n - RING)
                at_ = n % RING
                arrived = sum(2 if t[0] == "wo" else 1 for t in strips[at_:n + 1:RING])
                dve.wait_ge(w_raw_in[at_], 16 * arrived)
                dve.tensor_scalar(w_hi[:, at_], w_raw[:, at_], 1.0, 1.0, ALU.mult, ALU.mult)\
                    .then_inc(dve_hi_done, 1)
                dve.wait_ge(dve_hi_done, BY_DVE.index(n) + 1)
                dve.tensor_tensor(w_lo[:, at_], w_raw[:, at_], w_hi[:, at_].bitcast(F32), ALU.subtract)\
                    .then_inc(dve_split, 1)

            norm_x(0)
            split_strip(1)
            norm_x(1)
            for c in range(2, NT):
                low_hT(c - 2)
                norm_x(c)
            low_hT(NT - 2)
            low_hT(NT - 1)

            dve.wait_ge(rope_parts_in, 16 * 3)
            for n, g in enumerate((gq, gk)):
                dve.tensor_tensor(rope_t[:, n, 0, :, :], rope_in[:, 0, :, :],
                                  g[:, :].unsqueeze(1).to_broadcast([P, NT, HD]), ALU.mult)
                g_b = g[:, :].rearrange("p (a b i) -> p a b i", a=2, b=2)
                for b in range(2):
                    dst = rope_t[:, n, 1, :, :].rearrange("p c (a b i) -> p c a b i", a=2, b=2)[:, :, :, b, :]
                    src = rope_in[:, 1, :, :].rearrange("p c (a b i) -> p c a b i", a=2, b=2)[:, :, :, b, :]
                    last = dve.tensor_tensor(dst, src, g_b[:, :, 1 - b, :].unsqueeze(1)
                                             .to_broadcast([P, NT, 2, HD // 4]), ALU.mult)
            settle(last)

            NH = A_HEADS + A_KV
            dve.wait_ge(proj_read_act, 3 * NT)
            for c in range(NT):
                if c:
                    dve.wait_ge(a_sumsq, c)
                settle(dve.tensor_tensor(t1[:, :, :], zA[:, c], zA[:, c], ALU.mult))
                dve.tensor_reduce(ssqA[:, NH * c:NH * c + NH], t1[:, :, :], AX, ALU.add).then_inc(a_sumsq, 1)
            dve.wait_ge(a_sumsq, NT)
            for c in range(NT):
                dve.wait_ge(a_rstd, c + 1)
                settle(dve.tensor_tensor(zA[:, c], zA[:, c], rstdA[:, NH * c:NH * c + NH].unsqueeze(2)
                                         .to_broadcast([P, NH, HD]), ALU.mult))
                for n, h0, h1 in ((0, 0, A_HEADS), (1, A_HEADS, NH)):
                    nh = h1 - h0
                    dve.tensor_tensor(t1[:, h0:h1, :], zA[:, c, h0:h1, :],
                                      rope_t[:, n, 0, c, :].unsqueeze(1).to_broadcast([P, nh, HD]), ALU.mult)
                    z_b = zA[:, c, h0:h1, :].rearrange("p h (a b i) -> p h a b i", a=2, b=2)
                    t_b = t2[:, h0:h1, :].rearrange("p h (a b i) -> p h a b i", a=2, b=2)
                    s_b = rope_t[:, n, 1, c, :].rearrange("p (a b i) -> p a b i", a=2, b=2)
                    for b in range(2):
                        last = dve.tensor_tensor(t_b[:, :, :, b, :], z_b[:, :, :, 1 - b, :],
                                                 s_b[:, :, b, :].unsqueeze(1).to_broadcast([P, nh, 2, HD // 4]),
                                                 ALU.mult)
                settle(last)
                settle(dve.tensor_tensor(t1[:, :, :], t1[:, :, :], t2[:, :, :], ALU.add))
                if c >= 2:
                    dve.wait_ge(a_turned, 3 * (c - 1))
                q_hi, q_lo = q_parts[:, c % 2, :, 0, :], q_parts[:, c % 2, :, 1, :]
                k_p = k_parts[:, c % 2]
                dve.tensor_copy(q_hi, t1[:, 0:A_HEADS, :])
                dve.tensor_copy(k_p[:, :, 2, :], t1[:, A_HEADS:NH, :])
                settle(dve.tensor_copy(k_p[:, :, 0, :], t1[:, A_HEADS:NH, :]))
                dve.tensor_tensor(q_lo, t1[:, 0:A_HEADS, :], q_hi.bitcast(F32), ALU.subtract)
                dve.tensor_tensor(k_p[:, :, 1, :], t1[:, A_HEADS:NH, :], k_p[:, :, 0, :].bitcast(F32),
                                  ALU.subtract).then_inc(a_parts, 1)
                dve.wait_ge(a_parts, c + 1)

            def norm_probs(u, width):
                dve.wait_ge(exp_done, u + 1)
                settle(dve.reciprocal(column(rinv, u), column(rsum, u)))
                p = probs_of(u)[:, 0:width]
                dve.tensor_scalar(p, p, column(rinv, u), None, ALU.mult).then_inc(probs_normed, 1)

            def low_o(i):
                dve.wait_ge(o_hi_done, i + 1)
                dve.tensor_tensor(oT_lo[:, i, :], tp[2][:, :], oT_hi[:, i, :].bitcast(F32), ALU.subtract)\
                    .then_inc(o_lo_done, 1)

            def low_col(g, hh):
                _, kind, grp, hp = col_groups[g]
                dve.wait_ge(col_hi_done, 2 * g + hh + 1)
                src = bank[bank_of[N_TOK + g]]
                half = slice(HD * hh, HD * hh + HD)
                other = slice(HD - HD * hh, 2 * HD - HD * hh)
                if kind == "q":
                    q = q_of(hp, hh, grp)
                    last = dve.scalar_tensor_tensor(q[other, :], src[half, :], SCALE / SLOPES[2 * hp + hh],
                                                    q[half, :].bitcast(F32), ALU.mult, ALU.subtract)
                else:
                    hi = kB[half, hh, grp, 0, :].bitcast(F32)
                    dve.tensor_tensor(kB[other, hh, grp, 0, :], src[half, :], hi, ALU.subtract)
                    last = dve.tensor_tensor(kB[half, hh, grp, 1, :], src[half, :], hi, ALU.subtract)
                if hh:
                    last.then_inc(proj_read_dve, 1)

            for u in range(NA + 5):
                if u < NA:
                    dve.wait_ge(score_done, u + 1)
                    dve.tensor_reduce(column(nmax, u), pp[u % 3][:, :], AX, ALU.max, negate=True)\
                        .then_inc(nmax_done, 1)
                if 1 <= u <= NA:
                    norm_probs(u - 1, SEQ)
                for g in range(2 * NG):
                    for hh in range(2):
                        if u == filled_at(A_FILL, g) + 3 + hh:
                            low_col(g, hh)
                if u >= 12 and u % 8 == 4 and u < NA:
                    low_o(u // 8 - 1)
            low_o(OA - 1)

            dve.wait_ge(dist_in, 16)
            for hp in range(2):
                first, end = NA + 2 * NT * hp, NA + 2 * NT * (hp + 1)
                if hp:
                    for g in range(2 * NG + 2, 4 * NG):
                        low_col(g, 0)
                        low_col(g, 1)
                    low_o(OA)
                for u in range(first, end + 2):
                    if u < end:
                        head, c = divmod(u - NA, NT)
                        dve.wait_ge(score_done, u + 1)
                        wait_probs_free(dve, u)
                        dve.tensor_tensor_reduce(probs_of(u)[:, :], scores_two[u % 2], dist[:, c, :],
                                                 -SLOPES[head], HUGE, ALU.add, ALU.min,
                                                 column(nmax, u)).then_inc(nmax_done, 1)
                    if first < u <= end:
                        norm_probs(u - 1, SEQ + 2 * P)
                    if hp == 0:
                        for g in range(2):
                            if u == first + filled_at(B_FILL, g) + 3:
                                low_col(2 * NG + g, 0)
                                low_col(2 * NG + g, 1)
            low_o(OA + 1)

            for j in range(KC):
                if j:
                    dve.wait_ge(proj_read_act, N_TOK + 2 * (j + 1))
                else:
                    dve.wait_ge(first_gates_open, 2)
                dve.wait_ge(branch_done, 2 * (j + 1))
                if j:
                    dve.wait_ge(m_hi_done, j)
                    dve.wait_ge(m_lo_done, j)
                for b, m in enumerate((m_a, m_b)):
                    dve.tensor_tensor(m[:, :], stage_e[:, b, :], tp[2 * (j % 2) + b][:, :], ALU.mult)\
                        .then_inc(gates_used, 1)
                dve.wait_ge(gates_used, 2 * (j + 1))
                dve.tensor_tensor(m_a[:, :], m_a[:, :], m_b[:, :], ALU.add).then_inc(merged, 1)
                dve.wait_ge(m_hi_done, j + 1)
                dve.tensor_tensor(mT_lo[:, j, :], m_a[:, :], mT_hi[:, j, :].bitcast(F32), ALU.subtract)\
                    .then_inc(m_lo_done, 1)

            def add_residual(p, c):
                n = g_at[("res", p, c)]
                dve.wait_ge(proj_done, n + 1)
                part = x2[:, c, 2 * P * p:2 * P * (p + 1)]
                dve.tensor_tensor(part, part, bank[bank_of[n]][:, 0:2 * P], ALU.add).then_inc(proj_read_dve, 1)

            def norm_x2(c):
                dve.wait_ge(rstd2, c + 1)
                dve.tensor_scalar(xn[:, c, :], x2[:, c, :], rstd[:, c:c + 1], None, ALU.mult)\
                    .then_inc(xn_done, 1)

            def read_h2(c):
                dve.wait_ge(x2_turned, c + 1)
                if c >= 2:
                    dve.wait_ge(logits_done, c - 1)
                dve.tensor_copy(h2T[:, c % 2, HALF:KC, :],
                                tp[2 * (c % 2) + 1][:, :].rearrange("p (k i) -> p k i", i=P))\
                    .then_inc(h2T_dve_done, 1)

            def route_max(c):
                dve.wait_ge(logits_done, c + 1)
                settle(dve.tensor_reduce(smax[:, c:c + 1], bank[c][:, 0:NE], AX, ALU.max, negate=True))
                dve.wait_ge(rstd2, c + 1)
                dve.tensor_scalar(logit[:, c, :], bank[c][:, 0:NE], smax[:, c:c + 1], rstd[:, c:c + 1],
                                  ALU.add, ALU.mult).then_inc(smax_done, 1)

            def route_norm(c):
                dve.wait_ge(sexp_done, c + 1)
                settle(dve.reciprocal(sinv[:, c:c + 1], ssum[:, c:c + 1]))
                dve.tensor_scalar(aff[:, c, :], logit[:, c, :], sinv[:, c:c + 1], None, ALU.mult)\
                    .then_inc(aff_done, 1)

            dve.wait_ge(router_in, 16 * 2)
            dve.wait_ge(gains_in, 16 * 2)
            dve.tensor_tensor(w_rt[:, :, :], w_rt[:, :, :], g2.unsqueeze(2).to_broadcast([P, KC, NE]),
                              ALU.mult).then_inc(w_rt_scaled, 1)
            dve.wait_ge(x_again_in, 16)
            for group in groups[RES0:RES0 + 8]:
                add_residual(*group[1:])
            split_strip(len(strips) - 1)
            for group in groups[RES0 + 8:RES0 + 13]:
                add_residual(*group[1:])
            norm_x2(0)
            read_h2(0)
            add_residual(3, 2)
            norm_x2(1)
            read_h2(1)
            route_max(0)
            add_residual(2, 3)
            read_h2(2)
            route_norm(0)
            norm_x2(2)
            route_max(1)
            add_residual(3, 3)
            route_norm(1)
            dve.memset(zeros[0:NE, :], 0.0)
            read_h2(3)
            route_max(2)
            route_norm(2)
            route_max(3)
            route_norm(3)
            norm_x2(3)

            dve.wait_ge(route_turned, 1)
            settle(dve.tensor_copy(affT[0:NE, :].rearrange("e (i c) -> e c i", c=NT),
                                   bank[0][0:NE, :].rearrange("e (c i) -> e c i", c=NT)))
            row = affT[0:NE, :]
            for r in range(CAP // 8):
                eight = best[0:NE, 8 * r:8 * r + 8]
                settle(dve.max(eight, row))
                nxt = left[0:NE, r % 2, :]
                dve.match_replace(nxt, eight, row, -1.0).then_inc(eight_taken, 1)
                dve.wait_ge(eight_taken, r + 1)
                row = nxt
            settle(dve.tensor_scalar(taken[0:NE, :], row, 0.0, None, ALU.is_lt))
            settle(dve.tensor_tensor_scan(count[0:NE, :], taken[0:NE, :], zeros[0:NE, :], 0.0, ALU.add, ALU.add))
            dve.tensor_tensor(count[0:NE, :], count[0:NE, :], taken[0:NE, :], ALU.mult).then_inc(pos_done, 1)
            dve.wait_ge(route_turned, 2)
            dve.tensor_copy(pos[:, :, :], bank[1][:, 0:NT * NE].rearrange("p (c e) -> p c e", e=NE))\
                .then_inc(added, 1)
            dve.wait_ge(added, 1)

            def experts(q, first):
                wide = [P, NT, 2, CAP]
                place = slot_id[:, :].unsqueeze(1).unsqueeze(1).to_broadcast(wide)
                for pr in range(2):
                    own = pos[:, :, bass.ds(4 * q + 2 * pr, 2)].unsqueeze(3).to_broadcast(wide)
                    dve.tensor_tensor(pick[:, :, 2 * pr:2 * pr + 2, :], place, own, ALU.is_equal)\
                        .then_inc(pick_done, 1)

                def activate(i):
                    a = act[:, i % 2, :]
                    dve.wait_ge(sig_done, 4 * q + (i + 1))
                    dve.tensor_tensor(a, a, bank[4 * (i % 2)][:, :], ALU.mult).then_inc(silu_half, 1)
                    dve.wait_ge(silu_half, 4 * q + (i + 1))
                    m = half_at(i // 2, (w_up, 1, i % 2))
                    dve.wait_ge(w_slot_used[slot_of(first, m)], slot_round(first, q, m))
                    dve.tensor_tensor(a, a, bank[4 * (i % 2) + 1][:, :], ALU.mult).then_inc(act_done, 1)

                def low_y(pr):
                    for f in range(2):
                        dve.wait_ge(y_hi_done, 4 * q + (2 * pr + f + 1))
                        cols = slice(SEQ * f, SEQ * f + SEQ)
                        dve.scalar_tensor_tensor(y_lo[:, cols], bank[(3, 5)[f]][:, :], slot_aff[:, pr:pr + 1],
                                                 y_hi[:, cols].bitcast(F32), ALU.mult, ALU.subtract)\
                            .then_inc(y_lo_done, 1)

                def add(pr):
                    for n in range(8):
                        f, c = divmod(n, NT)
                        dve.wait_ge(scattered, 16 * q + (8 * pr + n + 1))
                        part = x2[:, c, SEQ * f:SEQ * f + SEQ]
                        dve.tensor_tensor(part, part, bank[6 + n % 2][:, :], ALU.add).then_inc(added, 1)

                dve.wait_ge(slot_aff_turned, q + 1)
                for e in range(2):
                    rows = slice(CAP * e, CAP * e + CAP)
                    dve.tensor_copy(slot_aff[rows, :],
                                    bank[2][rows, 0:4].rearrange("p (r e) -> p r e", e=2)[:, :, e])\
                        .then_inc(slot_aff_done, 1)
                activate(0)
                activate(1)
                for pr in range(2):
                    dve.wait_ge(give_turned, 2 * q + (pr + 1))
                    dve.tensor_copy(give[:, pr, :], bank[6 + pr][:, :]).then_inc(give_done, 1)
                low_y(0)
                activate(2)
                activate(3)
                add(0)
                low_y(1)
                add(1)

            experts(0, True)
            with dve.Fori(1, NE // 4) as q:
                experts(q, False)

            dve.wait_ge(gf_in, 16)
            for c in range(NT):
                dve.wait_ge(rstd3, c + 1)
                for f in range(2):
                    cols = slice(SEQ * f, SEQ * f + SEQ)
                    dve.scalar_tensor_tensor(fin[:, c, cols], x2[:, c, cols], rstd[:, c:c + 1], gf[:, cols],
                                             ALU.mult, ALU.mult).then_inc(fin_done, 1)


_INS = ["x", "norm1_g", "w_in", "b_gates", "q_norm_g", "k_norm_g", "w_o_a", "w_o_b", "w_out", "norm2_g",
        "w_router", "w_gate", "w_up", "w_down", "normf_g"]


def shape_constants():
    f = np.float32
    token = NT * np.arange(P)[:, None] + np.arange(NT)[None, :]
    half = HD // 2
    inv_freq = f(1.0) / (f(ROPE_THETA) ** (np.arange(0, half, 2, dtype=f) / f(half)))
    rope = np.zeros((P, 2, NT, 2, 2, HD // 4), f)
    for a, coord in enumerate((token // GRID_W, token % GRID_W)):
        angle = coord.astype(f)[..., None] * inv_freq
        rope[:, 0, :, a, :, :] = np.cos(angle)[:, :, None, :]
        rope[:, 1, :, a, 0, :] = -np.sin(angle)
        rope[:, 1, :, a, 1, :] = np.sin(angle)
    distance = np.zeros((P, NT, SEQ + 2 * P), f)
    i, j = np.arange(P)[:, None], np.arange(P)[None, :]
    for c in range(NT):
        for k in range(NT):
            far = np.abs(NT * (i - j) + c - k)
            distance[:, c, P * k:P * k + P] = -np.where(far <= B_GROUPS[0][0] // 2, far, FAR)
    for g in (1, 2):
        window, dil = B_GROUPS[g]
        far = NT * np.abs(i - j)
        share = SLOPES[g * B_HPG] / SLOPES[0]
        distance[:, :, SEQ + P * (g - 1):SEQ + P * g] = -np.where(
            (far <= window // 2) & (far % dil == 0), far * share, FAR)[:, None, :]
    slots = np.tile(np.arange(1, CAP + 1, dtype=f), (P, 1))
    return {"identity": np.eye(P, dtype=f), "rope": rope.reshape(P, 2, NT, HD), "distance": distance,
            "slots": slots}


def kernel(**inputs):
    import concourse.bacc as _bacc
    from concourse.bass_utils import run_bass_kernel_spmd as _run

    nc = _bacc.Bacc("TRN2", target_bir_lowering=False, num_devices=1)
    given = {name: np.ascontiguousarray(inputs[name]) for name in _INS} | shape_constants()
    arrays, args = {}, {}
    for name, a in given.items():
        arrays[f"in_{name}"] = a
        args[name] = nc.dram_tensor(f"in_{name}", a.shape, mybir.dt.from_np(a.dtype), kind="ExternalInput").ap()
    out = nc.dram_tensor("out", (1, SEQ, D), F32, kind="ExternalOutput").ap()
    encoder_block(nc, out=out, **args)
    r = _run(nc, [arrays], core_ids=[0])
    return r.results[0]["out"]
```
